# Optimizing a Trainium2 kernel written in Bass

```python
import functools
import jax
import jax.numpy as jnp
from jax import lax
import numpy as np

D_MODEL = 1024
BATCH = 1
SEQ = 256
DEPTH = 1

GRID_W = 64
CTX_LEN = 256
D_MIX = D_MODEL
GLA_WIDTH = D_MIX // 2
GLA_HEADS = 4
GLA_DV = GLA_WIDTH // GLA_HEADS
GLA_DK = GLA_DV // 2
GLA_QK = GLA_HEADS * GLA_DK
GATE_RANK = 16
GATE_NORMALIZER = 16.0
CHUNK = 64
CONV_WIDTH = D_MIX - GLA_WIDTH
CONV_K = 3
N_EXPERTS = 32
TOP_K = 4
D_FF = D_MODEL
SWIGLU_LIMIT = 7.0
SWIGLU_ALPHA = 1.702
MOE_BLOCK = 256
EPS = 1e-6

Q_END = GLA_QK
K_END = Q_END + GLA_QK
V_END = K_END + GLA_WIDTH
R_END = V_END + GLA_WIDTH
AF_END = R_END + GATE_RANK
AB_END = AF_END + GATE_RANK
B_END = AB_END + CONV_WIDTH
C_END = B_END + CONV_WIDTH
PROJ_WIDTH = C_END + CONV_WIDTH
PROJ_SPLITS = (Q_END, K_END, V_END, R_END, AF_END, AB_END, B_END, C_END)

kernel_name = 'hybrid_gla_shortconv_moe_dit'

def rms_norm(x, w):
    x32 = x.astype(jnp.float32)
    y = x32 * lax.rsqrt(jnp.mean(x32 * x32, axis=-1, keepdims=True) + EPS)
    return (y * w.astype(jnp.float32)).astype(x.dtype)

def modulate(x, shift, scale):
    return x * (1.0 + scale[:, None, :]) + shift[:, None, :]

def rev(t):
    return jnp.flip(t, axis=1)

def heads(t, d):
    bsz, length, _ = t.shape
    return t.reshape(bsz, length, GLA_HEADS, d).astype(jnp.float32)

def zero_state(bsz):
    return jnp.zeros((bsz, GLA_HEADS, GLA_DK, GLA_DV), jnp.float32)

def log_forget_gate(z_low, up, bias):
    bsz, length, _ = z_low.shape
    z = (z_low @ up + bias).astype(jnp.float32)
    return (jax.nn.log_sigmoid(z) / GATE_NORMALIZER).reshape(bsz, length, GLA_HEADS, GLA_DK)

def to_chunks(t):
    bsz, length, nh, d = t.shape
    return t.reshape(bsz, length // CHUNK, CHUNK, nh, d)

def gla_states(k, v, log_a, s0):
    k, v, log_a = to_chunks(k), to_chunks(v), to_chunks(log_a)
    b = jnp.cumsum(log_a, axis=2)
    b_end = b[:, :, -1]
    k_to_end = k * jnp.exp(b_end[:, :, None] - b)
    chunk_kv = jnp.einsum('bnshd,bnshv->bnhdv', k_to_end, v)
    decay = jnp.exp(b_end)

    def step(s, inp):
        dec, kv = inp
        return dec[..., None] * s + kv, s

    s_final, s_start = lax.scan(step, s0, (jnp.moveaxis(decay, 1, 0), jnp.moveaxis(chunk_kv, 1, 0)))
    return b, jnp.moveaxis(s_start, 0, 1), s_final

def gla_direction(q, k, v, log_a, s0):
    bsz, length = q.shape[:2]
    b, s_start, s_final = gla_states(k, v, log_a, s0)
    qc, kc, vc = to_chunks(q), to_chunks(k), to_chunks(v)
    q_dec = qc * jnp.exp(b)
    k_inv = kc * jnp.exp(-b)
    within = jnp.tril(jnp.ones((CHUNK, CHUNK), dtype=bool))
    scores = jnp.where(within, jnp.einsum('bnthd,bnshd->bnhts', q_dec, k_inv), 0.0)
    intra = jnp.einsum('bnhts,bnshv->bnthv', scores, vc)
    inter = jnp.einsum('bnthd,bnhdv->bnthv', q_dec, s_start)
    return (intra + inter).reshape(bsz, length, GLA_HEADS, GLA_DV), s_final

def gla_mixer(pq, pk, pv, pr, paf, pab, a_up_f, a_bias_f, a_up_b, a_bias_b, gla_norm_w, s0_f, s0_b):
    bsz, length = pq.shape[:2]
    q = heads(pq, GLA_DK) * (GLA_DK ** -0.5)
    k = heads(pk, GLA_DK)
    v = heads(pv, GLA_DV)
    la_f = log_forget_gate(paf, a_up_f, a_bias_f)
    la_b = log_forget_gate(pab, a_up_b, a_bias_b)
    o_f, s_f = gla_direction(q, k, v, la_f, s0_f)
    o_b, s_b = gla_direction(rev(q), rev(k), rev(v), rev(la_b), s0_b)
    o = rms_norm(o_f + rev(o_b), gla_norm_w)
    y = o.reshape(bsz, length, GLA_WIDTH) * jax.nn.silu(pr.astype(jnp.float32))
    return y.astype(pr.dtype), s_f, s_b

def depthwise_conv(u, w):
    return lax.conv_general_dilated(
        u, w[:, None, :].astype(u.dtype), window_strides=(1,), padding='SAME',
        dimension_numbers=('NWC', 'WIO', 'NWC'), feature_group_count=u.shape[-1])

def conv_rows(u, w, rows):
    bsz, length, ch = u.shape
    return depthwise_conv(u.reshape(bsz * rows, GRID_W, ch), w).reshape(bsz, length, ch)

def token_mixer(hn, conv_fn, s0_f, s0_b, w_in, a_up_f, a_bias_f, a_up_b, a_bias_b, gla_norm_w, conv_w, w_out):
    p = hn @ w_in
    pq, pk, pv, pr, paf, pab, p_b, p_c, p_x = jnp.split(p, PROJ_SPLITS, axis=-1)
    y_gla, s_f, s_b = gla_mixer(pq, pk, pv, pr, paf, pab, a_up_f, a_bias_f, a_up_b, a_bias_b,
                                gla_norm_w, s0_f, s0_b)
    y_conv = p_b * conv_fn(p_c * p_x, conv_w)
    y = jnp.concatenate([y_gla, y_conv], axis=-1) @ w_out
    return y, s_f, s_b

def context_states(hn, w_in, a_up_f, a_bias_f, a_up_b, a_bias_b):
    k = heads(hn @ w_in[:, Q_END:K_END], GLA_DK)
    v = heads(hn @ w_in[:, K_END:V_END], GLA_DV)
    la_f = log_forget_gate(hn @ w_in[:, R_END:AF_END], a_up_f, a_bias_f)
    la_b = log_forget_gate(hn @ w_in[:, AF_END:AB_END], a_up_b, a_bias_b)
    s0 = zero_state(hn.shape[0])
    s_f = gla_states(k, v, la_f, s0)[2]
    s_b = gla_states(rev(k), rev(v), rev(la_b), s0)[2]
    return s_f, s_b

def channel_mixer(hn, router_w, router_b, w_gu, b_gu, w_dn, b_dn):
    bsz, length, d = hn.shape
    xt = hn.reshape(-1, d)
    n_tok = xt.shape[0]
    logits = (xt @ router_w + router_b).astype(jnp.float32)
    top_val, top_idx = lax.top_k(logits, TOP_K)
    weights = jax.nn.softmax(top_val, axis=-1).astype(hn.dtype)
    flat_e = top_idx.reshape(-1)
    n_assign = n_tok * TOP_K
    order = jnp.argsort(flat_e)
    sorted_e = flat_e[order]
    sorted_tok = (order // TOP_K).astype(jnp.int32)
    sorted_w = weights.reshape(-1)[order]
    counts = jnp.bincount(flat_e, length=N_EXPERTS)
    padded = (counts + MOE_BLOCK - 1) // MOE_BLOCK * MOE_BLOCK
    pad_end = jnp.cumsum(padded)
    pad_start = pad_end - padded
    grp_start = jnp.cumsum(counts) - counts
    slot = pad_start[sorted_e] + (jnp.arange(n_assign) - grp_start[sorted_e])
    n_blocks = -(-n_assign // MOE_BLOCK) + N_EXPERTS
    n_slots = n_blocks * MOE_BLOCK
    slot_tok = jnp.full((n_slots,), n_tok, jnp.int32).at[slot].set(sorted_tok)
    slot_w = jnp.zeros((n_slots,), hn.dtype).at[slot].set(sorted_w)
    block_e = jnp.minimum(jnp.searchsorted(pad_end, jnp.arange(n_blocks) * MOE_BLOCK, side='right'),
                          N_EXPERTS - 1)
    x_pad = jnp.concatenate([xt, jnp.zeros((1, d), xt.dtype)], axis=0)

    def expert_block(args):
        tok, e = args
        gu = x_pad[tok] @ w_gu[e] + b_gu[e]
        gate = jnp.minimum(gu[:, 0::2], SWIGLU_LIMIT)
        up = jnp.clip(gu[:, 1::2], -SWIGLU_LIMIT, SWIGLU_LIMIT)
        act = (up + 1.0) * (gate * jax.nn.sigmoid(SWIGLU_ALPHA * gate))
        return act @ w_dn[e] + b_dn[e]

    y_slots = lax.map(expert_block, (slot_tok.reshape(n_blocks, MOE_BLOCK), block_e))
    y = jnp.zeros((n_tok + 1, d), hn.dtype).at[slot_tok].add(y_slots.reshape(n_slots, d) * slot_w[:, None])
    return y[:n_tok].reshape(bsz, length, d)

def setup_inputs(seed: int = 0) -> dict:
    key = jax.random.key(seed)
    ks = jax.random.split(key, 23)

    def nrm(k, shape, scale):
        return jax.random.normal(k, shape, jnp.float32) * scale

    return {
        'x': nrm(ks[0], (BATCH, SEQ, D_MODEL), 1.0),
        'c': nrm(ks[1], (BATCH, D_MODEL), 1.0),
        'ctx': nrm(ks[2], (BATCH, CTX_LEN, D_MODEL), 1.0),
        'c_ctx': nrm(ks[3], (D_MODEL,), 1.0),
        'w_ada': nrm(ks[4], (DEPTH, D_MODEL, 6 * D_MODEL), D_MODEL ** -0.5),
        'b_ada': nrm(ks[5], (DEPTH, 6 * D_MODEL), 0.01),
        'norm1_w': 1.0 + nrm(ks[6], (DEPTH, D_MODEL), 0.02),
        'w_in': nrm(ks[7], (DEPTH, D_MODEL, PROJ_WIDTH), D_MODEL ** -0.5),
        'a_up_f': nrm(ks[8], (DEPTH, GATE_RANK, GLA_QK), GATE_RANK ** -0.5),
        'a_bias_f': nrm(ks[9], (DEPTH, GLA_QK), 0.5),
        'a_up_b': nrm(ks[10], (DEPTH, GATE_RANK, GLA_QK), GATE_RANK ** -0.5),
        'a_bias_b': nrm(ks[11], (DEPTH, GLA_QK), 0.5),
        'gla_norm_w': 1.0 + nrm(ks[12], (DEPTH, GLA_DV), 0.02),
        'conv_w': nrm(ks[13], (DEPTH, CONV_K, CONV_WIDTH), CONV_K ** -0.5),
        'w_out': nrm(ks[14], (DEPTH, D_MIX, D_MODEL), D_MIX ** -0.5),
        'norm2_w': 1.0 + nrm(ks[15], (DEPTH, D_MODEL), 0.02),
        'router_w': nrm(ks[16], (DEPTH, D_MODEL, N_EXPERTS), D_MODEL ** -0.5),
        'router_b': nrm(ks[17], (DEPTH, N_EXPERTS), 0.01),
        'w_gu': nrm(ks[18], (DEPTH, N_EXPERTS, D_MODEL, 2 * D_FF), D_MODEL ** -0.5),
        'b_gu': nrm(ks[19], (DEPTH, N_EXPERTS, 2 * D_FF), 0.01),
        'w_dn': nrm(ks[20], (DEPTH, N_EXPERTS, D_FF, D_MODEL), D_FF ** -0.5),
        'b_dn': nrm(ks[21], (DEPTH, N_EXPERTS, D_MODEL), 0.01),
        'final_norm_w': 1.0 + nrm(ks[22], (D_MODEL,), 0.02),
    }

def reference(x, c, ctx, c_ctx, w_ada, b_ada, norm1_w, w_in, a_up_f, a_bias_f, a_up_b, a_bias_b,
              gla_norm_w, conv_w, w_out, norm2_w, router_w, router_b, w_gu, b_gu, w_dn, b_dn,
              final_norm_w):
    rows = x.shape[1] // GRID_W
    latent_conv = functools.partial(conv_rows, rows=rows)
    h, h_ctx = x, ctx
    for l in range(DEPTH):
        mix_w = (w_in[l], a_up_f[l], a_bias_f[l], a_up_b[l], a_bias_b[l], gla_norm_w[l], conv_w[l], w_out[l])
        moe_w = (router_w[l], router_b[l], w_gu[l], b_gu[l], w_dn[l], b_dn[l])
        mod = jax.nn.silu(c) @ w_ada[l] + b_ada[l]
        mod_ctx = (jax.nn.silu(c_ctx) @ w_ada[l] + b_ada[l])[None]
        sh1, sc1, g1, sh2, sc2, g2 = jnp.split(mod, 6, axis=-1)
        csh1, csc1, cg1, csh2, csc2, cg2 = jnp.split(mod_ctx, 6, axis=-1)
        last = l == DEPTH - 1

        hn_ctx = modulate(rms_norm(h_ctx, norm1_w[l]), csh1, csc1)
        if last:
            s_f, s_b = context_states(hn_ctx, *mix_w[:5])
        else:
            zs = zero_state(h_ctx.shape[0])
            y_ctx, s_f, s_b = token_mixer(hn_ctx, depthwise_conv, zs, zs, *mix_w)

        hn = modulate(rms_norm(h, norm1_w[l]), sh1, sc1)
        y, _, _ = token_mixer(hn, latent_conv, s_f, s_b, *mix_w)
        h = h + g1[:, None, :] * y
        h = h + g2[:, None, :] * channel_mixer(modulate(rms_norm(h, norm2_w[l]), sh2, sc2), *moe_w)

        if not last:
            h_ctx = h_ctx + cg1[:, None, :] * y_ctx
            h_ctx = h_ctx + cg2[:, None, :] * channel_mixer(
                modulate(rms_norm(h_ctx, norm2_w[l]), csh2, csc2), *moe_w)
    return rms_norm(h, final_norm_w)


_drawn_inputs = setup_inputs


def setup_inputs(seed=0):
    import zlib

    import numpy as np

    out = dict(_drawn_inputs(seed))
    spreads = {}
    factors = {'gla_norm_w': 10.329,
     'router_b': 11.22,
     'b_gu': 8.0,
     'b_dn': 29.017,
     'final_norm_w': 24.199,
     'norm2_w': 2.675}
    for name, (base, spread) in spreads.items():
        noise = np.random.default_rng([zlib.crc32(name.encode()), seed]).standard_normal(out[name].shape)
        drawn = base * np.exp(spread * noise) if base else spread * noise
        out[name] = jnp.asarray(drawn.astype(out[name].dtype))
    for name, factor in factors.items():
        out[name] = (out[name] * factor).astype(out[name].dtype)
    return out
```

```python
from contextlib import ExitStack

import concourse.bass as bass
from concourse import mybir

F32 = mybir.dt.float32
F32R = mybir.dt.float32r
BF16 = mybir.dt.bfloat16
I32 = mybir.dt.int32
U32 = mybir.dt.uint32
ALU = mybir.AluOpType
ACT = mybir.ActivationFunctionType
AX = mybir.AxisListType

P = 128
D = 1024
KC = D // P
NT = 512
SEQ = 256
GRID_W = 64
HEADS, DK, DV = 4, 64, 128
QK = HEADS * DK
GLA_W = HEADS * DV
CONV_W = D - GLA_W
RANK = 16
CH = 64
NCH = SEQ // CH
E = 32
TOPK = 4
FF = D
LIMIT, ALPHA, EPS = 7.0, 1.702, 1e-6
GATE_NORM = 16.0

Q0, V0, R0 = 0, 2 * QK, 2 * QK + GLA_W
AF0 = R0 + GLA_W
B0 = AF0 + 2 * RANK
C0, X0 = B0 + CONV_W, B0 + 2 * CONV_W

TOK = 64
ITEMS = E + (SEQ * TOPK - E) // TOK
ICOLS = ITEMS + 1
SLOTS = 6
GU, DN = 4, 2
SPLIT = 6
PIECE = SPLIT // 2
HI_BUFS = 3
WHOLE = KC - SPLIT

HEAD_TILES = ([("ada", c) for c in (0, 512, 1024, 1536)]
              + [("in", c) for c in (Q0, V0, R0, C0, X0, B0)]
              + [("ada", 2048 + NT * n) for n in range(8)]
              + [("out", 0), ("out", NT)])
NHEAD = len(HEAD_TILES)
FIRST_SLOT = (-NHEAD) % SLOTS


def head_slot(t):
    return (t + FIRST_SLOT) % SLOTS


def head_nth(t):
    return sum(head_slot(u) == head_slot(t) for u in range(t))


LAST_JOB = ([f"ada{a}" for a in range(4)] + ["qk3", "v3", "r1", "c1", "x1", "b1"]
            + [f"ada{a}" for a in range(4, 12)] + ["wo01", "wo11"])
HEAD_USES = [sum(head_slot(t) == j for t in range(NHEAD)) for j in range(SLOTS)]

JOBS = {}
BANK_USES = [0] * 8


def add_job(name, bank):
    JOBS[name] = (bank, BANK_USES[bank])
    BANK_USES[bank] += 1


def plan_jobs():
    JOBS.clear()
    BANK_USES[:] = [0] * 8
    turn = {}

    def job(name, banks):
        n = turn.get(banks, 0)
        turn[banks] = n + 1
        add_job(name, banks[n % len(banks)])

    job("cT", (7,))
    for t in range(4):
        job(f"ada{t}", (0, 1))
    for m in range(4):
        for half in range(2):
            job(f"hnT{m}{half}", (2, 3))
    job("aa", (7,))
    for g in range(4):
        job(f"qk{g}", (4, 5, 6))
    for g in range(4):
        job(f"z{g}", (2, 3))
    for g in range(4):
        job(f"v{g}", (4, 5, 6))
    for g in range(4):
        job(f"kp{g}", (2, 3))
    job("dec", (7,))
    for t in range(2):
        job(f"bT{t}", (2, 3))
    for t in range(2):
        job(f"r{t}", (4, 5, 6))
    for t in range(2):
        job(f"qkT{t}", (2, 3))
    for what in "cxb":
        for half in range(2):
            job(f"{what}{half}", (4, 5, 6))
    for s in range(7):
        job(f"kvf{s}", (2, 7))
        job(f"kvb{s}", (3, 6))
    for t in range(2):
        job(f"sce{t}", (2, 7))
        job(f"sco{t}", (3, 6))
    job("ada4", (0, 1))
    for t in range(2):
        job(f"oi{t}", (4, 5))
        job(f"oe{t}", (2, 7))
        job(f"oo{t}", (3, 6))
    for t in range(5, 9):
        job(f"ada{t}", (0, 1))
    for t in range(2):
        job(f"yT{t}", (2, 3))
    for t in range(9, 12):
        job(f"ada{t}", (0, 1))
    for half in range(2):
        for t in range(2):
            job(f"wo{half}{t}", (4, 5, 6))
    for t in range(2):
        for half in range(2):
            job(f"h2T{t}{half}", (2, 3))
    job("logits", (7,))
    job("rank", (0,))
    job("turn", (1,))
    job("start", (7,))
    job("items", (2,))
    job("bias0", (3,))
    job("bias1", (4,))


def hybrid_layer(nc, x, c, ctx_tok, c_ctx, w_ada, b_ada, norm1_w, w_in, a_up_f, a_bias_f, a_up_b, a_bias_b,
                 gla_norm_w, conv_w, w_out, norm2_w, router_w, router_b, w_gu, b_gu, w_dn, b_dn,
                 final_norm_w, out):
    plan_jobs()
    with ExitStack() as stack:
        base = (nc.sbuf_base + 63) // 64 * 64
        cursor = [base]

        def at(name, shape, dt=F32, offset=None):
            n = 4
            for s in shape[1:]:
                n *= s
            if dt == BF16:
                n //= 2
            n = (n + 31) // 32 * 32
            o = cursor[0] if offset is None else offset
            if offset is None:
                cursor[0] += n
            return nc.alloc_sbuf_tensor_at(name, shape, dt, offset=o)

        ring = at("ring", [P, SLOTS, KC, NT])
        ring_lo = [at(f"ring_lo{j}", [P, KC, NT], F32R, offset=base + 4 * KC * NT * j) for j in range(SLOTS)]
        hn2_at = cursor[0]
        hn2 = at("hn2", [P, 2, D])
        h1_at = cursor[0]
        h1 = at("h1", [P, 2, D])
        g2_at = cursor[0]
        g2_bc = at("g2_bc", [P, D])
        bias_items = at("bias_items", [P, 16, ICOLS])
        item_pos = at("item_pos", [P, 2, ICOLS])
        item_w = at("item_w", [P, 2, ICOLS])
        ident = at("ident", [P, P])
        slot_no = at("slot_no", [P, 2, TOK])
        ones = at("ones", [P, P])
        fold = at("fold", [P, TOK])
        table = at("table", [1, ICOLS + 1], I32)
        eps_col = at("eps_col", [P, 1])
        one_col = at("one_col", [P, 1])
        loop_at = cursor[0]
        xs = at("xs", [P, KC, 2 * TOK], F32R)
        gu_rows = at("gu_rows", [P, GU * NT])
        act_st = at("act_st", [P, KC, 2 * TOK], F32R)
        parts_at = cursor[0]
        hn2_parts = at("hn2_parts", [P, 2, 3, D], BF16)
        w_hi = at("w_hi", [P, HI_BUFS, 2, PIECE, NT], F32R)
        ident_bf = at("ident_bf", [P, P], BF16)
        y_hi = at("y_hi", [P, D], F32R)
        y_lo = at("y_lo", [P, D], F32R)
        pick = at("pick", [P, 2, 2 * TOK], BF16)
        pick_w = at("pick_w", [P, 2, 2 * TOK])
        put = at("put", [P, SEQ], F32R)
        slot_w = at("slot_w", [P, 1])
        gu_b = at("gu_b", [P, 2, 4, TOK])
        gu_c = at("gu_c", [P, 2, 4, TOK])
        sig = at("sig", [P, 2, 2, TOK])
        gated = at("gated", [P, 2, 2, TOK])
        act_full = at("act_full", [P, 2, 2, TOK])
        assert cursor[0] <= nc.sbuf_usable_end, (cursor[0], nc.sbuf_usable_end)

        cursor[0] = loop_at
        hnT_at = cursor[0]
        hnT = at("hnT", [P, 2, KC, SEQ])
        st_at = cursor[0]
        assert parts_at == st_at
        states = at("states", [P, 4, NCH, DV])
        mod = at("mod", [P, 2, D])
        resid = at("resid", [P, 2, D], offset=cursor[0])
        g1_bc = at("g1_bc", [P, D])
        norm_bc = at("norm_bc", [P, D])
        bias_at = cursor[0]
        ada_bias = at("ada_bias", [P, 2, NT])
        v_rows = at("v_rows", [P, 4, GLA_W])
        k_ctx = at("k_ctx", [P, 2, QK])
        yT = at("yT", [P, KC, SEQ])
        gate_at = cursor[0]
        aT = at("aT", [2 * RANK, 2 * SEQ])
        up_blk = at("up_blk", [2 * RANK, 2 * QK])
        a_bias = at("a_bias", [P, 2 * QK])
        la_at = cursor[0]
        la = at("la", [P, 4, 2 * QK])
        cmix_at = cursor[0]
        c_mix = at("c_mix", [P, KC, 2, 64])
        call_at = cursor[0]
        c_all = at("c_all", [P, KC, P])
        tri = at("tri", [P, P])
        up_to = at("up_to", [P, 2, P], offset=g2_at)
        beyond = at("beyond", [P, 2, P], offset=g2_at + 1024)
        in_chunk = at("in_chunk", [P, 2])
        glan_bc = at("glan_bc", [P, DV], offset=g2_at + 2048)
        w_aa = at("w_aa", [P, KC, 2 * RANK], offset=g2_at + 2560)
        conv_k = at("conv_k", [P, 3, CONV_W // P])
        c_rows = at("c_rows", [2 * KC, P])
        c_sig = at("c_sig", [2 * KC, P])
        sums = at("sums", [P, 16])
        rstd = at("rstd", [P, 16])
        decay = at("decay", [P, 4, 2 * NCH])
        assert cursor[0] <= nc.sbuf_usable_end, (cursor[0], nc.sbuf_usable_end)
        x_mix = at("x_mix", [P, 4, D], offset=hn2_at)
        k_end = at("k_end", [P, 4, 2, QK], offset=hn2_at)
        r_rows = at("r_rows", [P, 2, GLA_W], offset=h1_at)
        qk_rows = at("qk_rows", [P, 2, 2 * QK], offset=h1_at + 4096)
        q_dec = at("q_dec", [P, 4, SEQ], offset=la_at)
        k_inv = at("k_inv", [P, 4, SEQ], offset=la_at + 4096)
        scores = at("scores", [P, 2, HEADS, 2, CH], offset=cmix_at)
        conv_u = at("conv_u", [P, 4, SEQ], offset=hnT_at + 8192)
        conv_y = at("conv_y", [P, 4, SEQ], offset=hnT_at + 12288)
        o_rows = at("o_rows", [P, 2, GLA_W], offset=hnT_at + 8192)
        o_sq = at("o_sq", [P, 2, GLA_W], offset=hnT_at + 12288)
        keep = at("keep", [P, HEADS, 2, CH], offset=gate_at)
        scaled = at("scaled", [P, GLA_W], offset=gate_at + 2048)
        h2T = at("h2T", [P, KC, SEQ], offset=hnT_at)
        bgu_rows = at("bgu_rows", [E, 2 * FF], offset=hnT_at + 8192)
        bdn_rows = at("bdn_rows", [E, D], offset=call_at)
        r_w = at("r_w", [P, KC, E], offset=cmix_at)
        rt_at = cmix_at + 1024
        r_b = at("r_b", [P, E], offset=rt_at)
        logit = at("logit", [P, 2, E], offset=rt_at + 128)
        top = at("top", [P, 2, 8], offset=rt_at + 384)
        top_i = at("top_i", [P, 2, 8], U32, offset=rt_at + 448)
        top_f = at("top_f", [P, 2, TOPK], offset=rt_at + 512)
        soft = at("soft", [P, 2, TOPK], offset=rt_at + 544)
        soft_s = at("soft_s", [P, 2], offset=rt_at + 576)
        soft_r = at("soft_r", [P, 2], offset=rt_at + 608)
        w_top = at("w_top", [P, 2, TOPK], offset=rt_at + 640)
        sel = at("sel", [P, 2, E], offset=rt_at + 672)
        w_full = at("w_full", [P, 2, E], offset=rt_at + 928)
        pos = at("pos", [P, 2, E], offset=rt_at + 1184)
        e_no = at("e_no", [P, E], offset=rt_at + 1440)
        i_no = at("i_no", [P, ICOLS], offset=rt_at + 1568)
        i_no64 = at("i_no64", [P, ICOLS], offset=rt_at + 1792)
        limits = at("limits", [E, 3], offset=rt_at + 2016)
        more = at("more", [E, 3], offset=rt_at + 2048)
        tiles_e = at("tiles_e", [E, 1], offset=rt_at + 2080)
        begin_e = at("begin_e", [E, 4], offset=rt_at + 2112)
        e_col = at("e_col", [E, 1], offset=rt_at + 2144)
        below = at("below", [E, E], offset=rt_at + 2176)
        own = at("own", [E, ICOLS], offset=rt_at + 2304)
        hot = at("hot", [P, 2, TOPK, E], offset=bias_at)
        hot_w = at("hot_w", [P, 2, TOPK, E], offset=bias_at + 1024)
        routeT = at("routeT", [E, 2, SEQ], offset=bias_at + 2048)
        fin_n = at("fin_n", [P, D], offset=base)
        fin_y = at("fin_y", [P, 2, D], offset=base + 4096)
        fin_sq = at("fin_sq", [P, 2, D], offset=base + 12288)

        sums_f = at("sums_f", [P, 2], offset=base + 20480)
        rstd_f = at("rstd_f", [P, 2], offset=base + 20512)

        bank = [stack.enter_context(nc.psum_tensor(f"bank{b}", [P, NT], F32)) for b in range(8)]
        acc = bank[0:4]
        mm = bank[4:6]
        fold_ps = bank[6]
        gather_ps = bank[7]

        def sem(name):
            return stack.enter_context(nc.semaphore(name))

        def sems(name, n):
            return [sem(f"{name}{i}") for i in range(n)]

        landed = sems("landed", SLOTS)
        used = sems("used", SLOTS)
        full = sems("bank_full", 8)
        read = sems("bank_read", 8)
        l_c, l_x, l_norm, l_aa, l_up, l_abias, l_glan, l_conv = (
            sem(f"load_{n}") for n in ("c", "x", "norm", "aa", "up", "abias", "glan", "conv"))
        l_bias = sems("load_ada_bias", 2)
        l_xres, l_norm2, l_router, l_bgu, l_bdn, l_fin, stored = (
            sem(n) for n in ("load_xres", "load_norm2", "load_router", "load_bgu", "load_bdn", "load_fin", "stored"))
        pool_step = sem("pool_step")
        step, at_step = [0], {}
        c_sigd, c_silud, c_ready = sem("c_sigmoid"), sem("c_silu"), sem("c_cols")
        ada_used = sem("ada_bias_used")
        mod_ready = sem("mod_ready")
        sq_done, rs_sqrt, rs_done, hn_step, hn_ready = (
            sem(n) for n in ("squares", "roots", "rstd_ready", "hn_scaled", "hn_ready"))
        z_step, e_step, ln_step, la_ready = (sem(n) for n in ("z_step", "exp_step", "ln_step", "la_ready"))
        k_ready, bx, qd_ready = sem("k_end_ready"), sem("b_exp"), sem("qk_decayed")
        conv_step, yconv, st_step, sc_zero = (
            sem(n) for n in ("conv_step", "y_conv", "state_step", "scores_zeroed"))
        o_step, o_sum, o_root, r_sig, r_silu, y_ready = (
            sem(n) for n in ("o_step", "o_sum", "o_root", "r_sigmoid", "r_silu", "y_rows"))
        h1_ready, h_sq, h_root, h_step, hn2_ready = (
            sem(n) for n in ("h1_ready", "h_sq", "h_root", "h_step", "hn2_ready"))
        rt, rt_exp, rt_sel, rt_pos, rt_own, rt_T, tab_ready, it_ready = (
            sem(n) for n in ("route_step", "route_exp", "selected", "positions", "owners", "routeT_ready",
                             "table_ready", "items_ready"))
        part_a, part_r, part_b, part_c = sem("part_0"), sem("part_0_rest"), sem("part_1"), sem("part_2")
        acc_open = sem("acc_open")
        hi_done, lo_done = sem("w_hi_done"), sem("w_lo_done")
        rows_out, folded = sem("gu_rows_out"), sem("folded")
        biased, gate_c, up_c, sig_done, gated_s, actf, acth, act_ready = (
            sem(n) for n in ("gu_biased", "gate_clamped", "up_clamped", "sigmoid", "gated", "act_full",
                                  "act_hi", "act_ready"))
        scattered, turned, put_ready, slot_w_ready = (
            sem(n) for n in ("scattered", "pick_turned", "put_ready", "slot_w_ready"))
        pick_ready, pickw_ready = sem("pick_ready"), sem("pick_w_ready")
        gathered, xs_hi_s, xs_ready = sem("gathered"), sem("xs_hi_ready"), sem("xs_ready")
        yhi_s, ylo_s = sems("y_hi_ready", 2), sems("y_lo_ready", 2)
        f_step, f_sq, f_root = sem("final_step"), sem("final_sq"), sem("final_root")

        def await_bank(eng, name):
            b, n = JOBS[name]
            if n:
                eng.wait_ge(read[b], n)
            return bank[b]

        def await_job(eng, name):
            b, n = JOBS[name]
            eng.wait_ge(full[b], n + 1)
            return bank[b]

        def after_job(eng, name):
            b, n = JOBS[name]
            eng.wait_ge(full[b], n + 1)

        def filled(ins, name):
            ins.then_inc(full[JOBS[name][0]], 1)

        def was_read(ins, name):
            ins.then_inc(read[JOBS[name][0]], 1)

        def after_read(eng, name):
            b, n = JOBS[name]
            eng.wait_ge(read[b], n + 1)

        def tok(g):
            return lambda k: hnT[:, g // 2, k, (g % 2) * P:(g % 2 + 1) * P]

        block = stack.enter_context(nc.Block())

        @block.sync
        def _(sp):
            source = {"ada": w_ada[0], "in": w_in[0], "out": w_out[0]}
            for t, (what, col) in enumerate(HEAD_TILES):
                j, n = head_slot(t), head_nth(t)
                if n:
                    after_job(sp, LAST_JOB[t - SLOTS])
                sp.dma_start(ring[:, j], source[what].rearrange("(k p) n -> p k n", p=P)[:, :, col:col + NT])\
                    .then_inc(landed[j], 16)
            for j in range(SLOTS):
                after_job(sp, LAST_JOB[NHEAD - SLOTS + j])
                w, col = (w_gu, NT * j) if j < GU else (w_dn, NT * (j - GU))
                sp.dma_start(ring[:, j], w[0, 0].rearrange("(k p) n -> p k n", p=P)[:, :, col:col + NT])\
                    .then_inc(landed[j], 16)
            sp.wait_ge(tab_ready, 1)
            n_items = sp.value_load(table[0:1, ICOLS:ICOLS + 1], min_val=1, max_val=ITEMS)
            with sp.Fori(1, ITEMS) as i:
                with sp.If(i < n_items):
                    e = sp.value_load(table[0:1, bass.ds(i, 1)], min_val=0, max_val=E - 1)
                    for j in range(SLOTS):
                        w = w_gu if j < GU else w_dn
                        col = NT * (j if j < GU else j - GU)
                        sp.wait_ge(used[j], i + 1)
                        sp.dma_start(ring[:, j], w[0][bass.ds(e, 1)].rearrange("e (k p) n -> p (e k) n", p=P)
                                     [:, :, col:col + NT]).then_inc(landed[j], 16)
            for j in range(SLOTS):
                sp.wait_ge(used[j], n_items + 1)
            sp.dma_start(fin_n[:, :], final_norm_w.partition_broadcast(P)).then_inc(l_fin, 16)
            for t in range(2):
                sp.wait_ge(f_step, 10 + t)
                sp.dma_start(out[0, t * P:(t + 1) * P, :], fin_y[:, t, :]).then_inc(stored, 16)
            sp.wait_ge(stored, 32)

        @block.gpsimd
        def _(pool):
            def made(ins, name=None):
                step[0] += 1
                ins.then_inc(pool_step, 1)
                pool.wait_ge(pool_step, step[0])
                if name:
                    at_step[name] = step[0]

            def select(view, op, base_, pattern, mult, fill):
                return pool.affine_select(out=view, in_=view, compare_op=op, fill=fill, base=base_,
                                          pattern=pattern, channel_multiplier=mult)

            made(pool.memset(ident[:, :], 0.0))
            made(pool.memset(ones[:, :], 1.0))
            made(pool.memset(eps_col[:, :], EPS))
            made(pool.memset(one_col[:, :], 1.0))
            made(select(ident[:, :], ALU.not_equal, 0, [[-1, P]], 1, 1.0), "ident")
            for t in range(2):
                pool.dma_start(ada_bias[:, t, :], b_ada[0, t * NT:(t + 1) * NT].partition_broadcast(P))\
                    .then_inc(l_bias[t], 16)
            pool.dma_start(norm_bc[:, :], norm1_w[0].partition_broadcast(P)).then_inc(l_norm, 16)
            pool.dma_start(w_aa[:, :, :], w_in[0].rearrange("(k p) n -> p k n", p=P)[:, :, AF0:AF0 + 2 * RANK])\
                .then_inc(l_aa, 16)
            made(pool.memset(up_blk[:, :], 0.0))
            pool.dma_start(up_blk[0:RANK, 0:QK], a_up_f[0]).then_inc(l_up, 16)
            pool.dma_start(up_blk[RANK:2 * RANK, QK:2 * QK], a_up_b[0]).then_inc(l_up, 16)
            pool.dma_start(a_bias[:, 0:QK], a_bias_f[0].partition_broadcast(P)).then_inc(l_abias, 16)
            pool.dma_start(a_bias[:, QK:2 * QK], a_bias_b[0].partition_broadcast(P)).then_inc(l_abias, 16)
            pool.dma_start(glan_bc[:, :], gla_norm_w[0].partition_broadcast(P)).then_inc(l_glan, 16)
            for m in (up_to, beyond):
                made(pool.memset(m[:, :, :], 1.0 / GATE_NORM))
            made(pool.memset(in_chunk[:, :], 0.0))
            made(select(up_to[:, 0, :], ALU.is_ge, 0, [[1, P]], -1, 0.0))
            made(select(up_to[:, 1, :], ALU.is_ge, 0, [[-1, P]], 1, 0.0))
            made(select(beyond[:, 0, :], ALU.is_gt, 0, [[-1, P]], 1, 0.0))
            made(select(beyond[:, 1, :], ALU.is_gt, 0, [[1, P]], -1, 0.0))
            for m in (up_to, beyond):
                made(pool.memset(m[0:CH, :, CH:P], 0.0))
                made(pool.memset(m[CH:P, :, 0:CH], 0.0))
            made(pool.memset(in_chunk[0:CH, 0:1], 1.0 / GATE_NORM))
            made(pool.memset(in_chunk[CH:P, 1:2], 1.0 / GATE_NORM))
            made(pool.iota(slot_no[:, :, :], pattern=[[0, 2], [1, TOK]], base=1, channel_multiplier=0,
                      allow_small_or_imprecise_dtypes=True))
            made(pool.memset(fold[:, :], 0.0))
            for half in range(2):
                rows = fold[half * TOK:(half + 1) * TOK, :]
                made(select(rows, ALU.not_equal, 0, [[-1, TOK]], 1, 1.0), "scan")
            with nc.allow_non_contiguous_dma(reason="conv taps, by channel"):
                for tap in range(3):
                    pool.dma_start(conv_k[:, tap, :], conv_w[0, tap].rearrange("(f p) -> p f", p=P))\
                        .then_inc(l_conv, 16)
            for t in range(2, 12):
                pool.wait_ge(ada_used, t - 1)
                pool.dma_start(ada_bias[:, t % 2, :], b_ada[0, t * NT:(t + 1) * NT].partition_broadcast(P))\
                    .then_inc(l_bias[t % 2], 16)
                if t == 5:
                    pool.wait_ge(mod_ready, 1)
                    pool.dma_start(norm_bc[:, :], norm2_w[0].partition_broadcast(P)).then_inc(l_norm2, 16)
                    pool.wait_ge(z_step, 4)
                    made(pool.memset(keep[:, :, :, :], 1.0))
                    for half in range(2):
                        rows = keep[half * CH:(half + 1) * CH]
                        made(select(rows[:, :, 0, :], ALU.is_ge, 0, [[0, HEADS], [1, CH]], -1, 0.0))
                        made(select(rows[:, :, 1, :], ALU.is_ge, 0, [[0, HEADS], [-1, CH]], 1, 0.0), "keep")
            pool.wait_ge(y_ready, 2)
            pool.dma_start(h1[:, :, :], x[0].rearrange("(t p) n -> p t n", p=P)).then_inc(l_xres, 16)
            after_job(pool, "yT1")
            pool.dma_start(bgu_rows[:, :], b_gu[0]).then_inc(l_bgu, 16)
            pool.wait_ge(ada_used, 12)
            pool.dma_start(bdn_rows[:, :], b_dn[0]).then_inc(l_bdn, 16)
            pool.dma_start(r_w[:, :, :], router_w[0].rearrange("(k p) e -> p k e", p=P)).then_inc(l_router, 16)
            pool.dma_start(r_b[:, :], router_b[0].partition_broadcast(P)).then_inc(l_router, 16)
            exact = dict(allow_small_or_imprecise_dtypes=True)
            made(pool.iota(e_no[:, :], pattern=[[1, E]], base=0, channel_multiplier=0, **exact))
            made(pool.iota(i_no[:, :], pattern=[[1, ICOLS]], base=0, channel_multiplier=0, **exact))
            made(pool.iota(i_no64[:, :], pattern=[[TOK, ICOLS]], base=0, channel_multiplier=0, **exact))
            made(pool.iota(limits[:, :], pattern=[[TOK, 3]], base=TOK, channel_multiplier=0, **exact))
            made(pool.iota(e_col[:, :], pattern=[[0, 1]], base=0, channel_multiplier=1, **exact))
            made(pool.memset(below[:, :], 1.0))
            made(pool.memset(tri[:, :], 1.0))
            made(select(below[:, :], ALU.is_gt, 0, [[1, E]], -1, 0.0))
            made(select(tri[:, :], ALU.is_ge, 0, [[1, P]], -1, 0.0), "tables")

        @block.scalar
        def _(act):
            def copy(o, i):
                return act.activation(o, i, ACT.Copy)

            act.dma_start(c_rows[0:KC, :], c[0].rearrange("(k p) -> k p", p=P)).then_inc(l_c, 16)
            act.dma_start(c_rows[KC:2 * KC, :], c_ctx.rearrange("(k p) -> k p", p=P)).then_inc(l_c, 16)
            for half, src in enumerate((x, ctx_tok)):
                act.dma_start(x_mix[half * 64:half * 64 + 64], src[0].rearrange("(m p) n -> p m n", p=64))\
                    .then_inc(l_x, 16)
            act.wait_ge(l_c, 32)
            act.activation(c_sig[:, :], c_rows[:, :], ACT.Sigmoid).then_inc(c_sigd, 1)
            act.wait_ge(l_x, 32)
            for m in range(4):
                act.activation(hnT[:, 0, 4 * (m % 2):4 * (m % 2) + 4, :], x_mix[:, m, :].rearrange("p (a b) -> p a b", a=4),
                               ACT.Square, accum_out=sums[:, m:m + 1]).then_inc(sq_done, 1)
                act.wait_ge(sq_done, m + 1)
            act.wait_ge(pool_step, at_step["ident"])
            act.activation(rstd[:, 0:4], sums[:, 0:4], ACT.Sqrt, bias=eps_col[:, 0:1], scale=1.0 / D)\
                .then_inc(rs_sqrt, 1)
            for m in range(4):
                for half in range(2):
                    ps = await_job(act, f"hnT{m}{half}")
                    src = ps[:, :].rearrange("p (k s t) -> p s k t", k=4, s=2)
                    for s in range(2):
                        ins = copy(hnT[:, s, 4 * half:4 * half + 4, m * 64:(m + 1) * 64], src[:, s])
                        if s:
                            was_read(ins, f"hnT{m}{half}")
            ps = await_job(act, "aa")
            was_read(copy(aT[:, :], ps[0:2 * RANK, :]), "aa")
            for g in range(4):
                ps = await_job(act, f"qk{g}")
                if g < 2:
                    was_read(copy(qk_rows[:, g, :], ps[:, :]), f"qk{g}")
                else:
                    was_read(copy(k_ctx[:, g - 2, :], ps[:, 0:QK]), f"qk{g}")
            for g in range(4):
                act.wait_ge(z_step, 4 + g + 1)
                act.activation(la[:, g, :], la[:, g, :], ACT.Exp).then_inc(e_step, 1)
            for g in range(4):
                act.wait_ge(e_step, g + 1)
                act.activation(la[:, g, :], la[:, g, :], ACT.Ln, bias=one_col[:, 0:1]).then_inc(ln_step, 1)
            for g in range(4):
                ps = await_job(act, f"v{g}")
                was_read(copy(v_rows[:, g, :], ps[:, :]), f"v{g}")
            for g in range(4):
                ps = await_job(act, f"kp{g}")
                was_read(act.activation(k_end[:, g], ps[:, :].rearrange("p (d n) -> p d n", d=2), ACT.Exp), f"kp{g}")
            ps = await_job(act, "dec")
            was_read(act.activation(decay[:, :, :].rearrange("p d (g h) -> p d g h", g=4), ps[:, 0:32].rearrange("p (g dp h) -> p dp g h", g=4, dp=4),
                                    ACT.Exp), "dec")
            for t in range(2):
                ps = await_job(act, f"bT{t}")
                src = ps[:, :].rearrange("p (d t) -> p d t", d=4)
                if t == 0:
                    act.wait_ge(full[JOBS["bT1"][0]], JOBS["bT1"][1] + 1)
                act.activation(q_dec[:, :, t * P:(t + 1) * P], src, ACT.Exp).then_inc(bx, 1)
                was_read(act.activation(k_inv[:, :, t * P:(t + 1) * P], src, ACT.Exp, scale=-1.0), f"bT{t}")
            for t in range(2):
                ps = await_job(act, f"r{t}")
                was_read(copy(r_rows[:, t, :], ps[:, :]), f"r{t}")
            for half in range(2):
                ps = await_job(act, f"c{half}")
                was_read(copy(conv_u[:, 2 * half:2 * half + 2, :], ps[:, :].rearrange("p (f t) -> p f t", f=2)),
                         f"c{half}")
            for t in range(2):
                ps = await_job(act, f"oi{t}")
                if t == 0:
                    act.wait_ge(yconv, 2)
                was_read(copy(o_rows[:, t, :], ps[:, :]), f"oi{t}")
            act.wait_ge(o_sum, 2)
            act.activation(rstd[:, 4:12], sums[:, 4:12], ACT.Sqrt, bias=eps_col[:, 0:1], scale=1.0 / DV)\
                .then_inc(o_root, 1)
            for t in range(2):
                act.activation(o_sq[:, t, :], r_rows[:, t, :], ACT.Sigmoid).then_inc(r_sig, 1)
            for t in range(2):
                ps = await_job(act, f"yT{t}")
                was_read(copy(yT[:, 0:4, t * P:(t + 1) * P], ps[:, :].rearrange("p (f t) -> p f t", f=4)), f"yT{t}")
            for t in range(2):
                act.wait_ge(h1_ready, 4)
                act.activation(hn2[:, t, :], h1[:, t, :], ACT.Square, accum_out=sums[:, 12 + t:13 + t])\
                    .then_inc(h_sq, 1)
            act.wait_ge(h_sq, 2)
            act.activation(rstd[:, 12:14], sums[:, 12:14], ACT.Sqrt, bias=eps_col[:, 0:1], scale=1.0 / D)\
                .then_inc(h_root, 1)
            for t in range(2):
                act.wait_ge(hn2_ready, t + 1)
                copy(hn2_parts[:, t, 0, :], hn2[:, t, :]).then_inc(part_a, 1)
                for half in range(2):
                    ps = await_job(act, f"h2T{t}{half}")
                    was_read(copy(h2T[:, 4 * half:4 * half + 4, t * P:(t + 1) * P],
                                  ps[:, :].rearrange("p (k t) -> p k t", k=4)), f"h2T{t}{half}")
            act.wait_ge(rt, 3)
            act.activation(soft[:, :, :], soft[:, :, :], ACT.Exp).then_inc(rt_exp, 1)
            for t in range(2):
                act.wait_ge(part_r, t + 1)
                copy(hn2_parts[:, t, 1, :], resid[:, t, :]).then_inc(part_b, 1)
            for half in range(2):
                ps = await_job(act, f"bias{half}")
                was_read(copy(bias_items[:, 8 * half:8 * half + 8, :],
                              ps[:, 0:8 * ICOLS].rearrange("p (f i) -> p f i", f=8)), f"bias{half}")

            def xs_first():
                copy(xs[:, :, 0:TOK], gather_ps[:, :].rearrange("p (k m) -> p k m", k=KC)).then_inc(xs_hi_s, 1)

            def y_first(h):
                act.activation(y_hi[:, h * NT:(h + 1) * NT], mm[h][:, :], ACT.Copy, scale=slot_w[:, 0:1])\
                    .then_inc(yhi_s[h], 1)

            act.wait_ge(gathered, 1)
            xs_first()
            act.activation(sig[:, 0], gu_c[:, 0, 0:2, :], ACT.Sigmoid, scale=ALPHA)
            act.wait_ge(tab_ready, 1)
            n_items = act.value_load(table[0:1, ICOLS:ICOLS + 1], min_val=1, max_val=ITEMS)
            with act.Fori(0, ITEMS) as i:
                with act.If(i < n_items):
                    i4 = act.snap(i * GU)

                    def halve(j):
                        act.wait_ge(landed[j], 16 * (i + HEAD_USES[j] + 1))
                        b = (j - HI_BUFS) % SLOTS
                        act.wait_ge(used[b], i + (2 if j >= HI_BUFS else 1))
                        for p in range(2):
                            k = WHOLE + p * PIECE
                            copy(w_hi[:, j % HI_BUFS, p], ring[:, j, k:k + PIECE, :]).then_inc(hi_done, 1)

                    def rows(j):
                        act.wait_ge(used[j], i + 2)
                        copy(gu_rows[:, j * NT:(j + 1) * NT], mm[j % 2][:, :]).then_inc(rows_out, 1)

                    def sigmoid(j):
                        act.wait_ge(gate_c, i4 + j + 1)
                        act.activation(sig[:, j % 2], gu_c[:, j % 2, 0:2, :], ACT.Sigmoid, scale=ALPHA)\
                            .then_inc(sig_done, 1)

                    halve(0)
                    halve(1)
                    act.wait_ge(used[5], i + 1)
                    y_first(1)
                    halve(2)
                    rows(0)
                    halve(3)
                    rows(1)
                    sigmoid(0)
                    halve(4)
                    rows(2)
                    sigmoid(1)
                    sigmoid(2)
                    halve(5)
                    rows(3)
                    sigmoid(3)
                    act.wait_ge(gathered, i + 2)
                    xs_first()
                    act.wait_ge(used[4], i + 2)
                    act.wait_ge(slot_w_ready, i + 2)
                    y_first(0)
            for j in range(SLOTS):
                act.wait_ge(used[j], n_items + 1)
            y_first(1)
            for t in range(2):
                act.wait_ge(f_step, 4 * (t + 1))
                act.activation(fin_sq[:, t, :], fin_y[:, t, :], ACT.Square, accum_out=sums_f[:, t:t + 1])\
                    .then_inc(f_sq, 1)
            act.wait_ge(f_sq, 2)
            act.activation(rstd_f[:, 0:2], sums_f[:, 0:2], ACT.Sqrt, bias=eps_col[:, 0:1], scale=1.0 / D)\
                .then_inc(f_root, 1)

        @block.vector
        def _(dve):
            dve.wait_ge(c_sigd, 1)
            dve.tensor_tensor(c_rows[:, :], c_rows[:, :], c_sig[:, :], ALU.mult).then_inc(c_silud, 1)
            ps = await_job(dve, "cT")
            dve.tensor_copy(c_mix[:, :, :, :], ps[:, 0:2 * KC].rearrange("p (s k) -> p k s", s=2)
                            .unsqueeze(3).broadcast_to([P, KC, 2, 64])).then_inc(c_ready, 1)
            was_read(dve.tensor_copy(c_all[:, :, :], ps[:, 0:KC].unsqueeze(2).broadcast_to([P, KC, P])), "cT")

            def bias_landed(t):
                dve.wait_ge(l_bias[t % 2], 16 * (t // 2 + 1))

            def ada_add(t, dst):
                ps = await_job(dve, f"ada{t}")
                bias_landed(t)
                was_read(dve.tensor_tensor(dst, ps[:, :], ada_bias[:, t % 2, :], ALU.add), f"ada{t}")
                after_read(dve, f"ada{t}")
                dve.engine_nop().then_inc(ada_used, 1)

            def ada_scale(t, dst, cols):
                ps = await_job(dve, f"ada{t}")
                bias_landed(t)
                was_read(dve.scalar_tensor_tensor(out=dst, in0=ps[:, :], scalar=1.0, in1=ada_bias[:, t % 2, :],
                                                  op0=ALU.add, op1=ALU.add), f"ada{t}")
                after_read(dve, f"ada{t}")
                ins = dve.tensor_tensor(dst, dst, norm_bc[:, cols], ALU.mult)
                ins.then_inc(ada_used, 1)

            for t in range(2):
                ada_add(t, mod[:, 1, t * NT:(t + 1) * NT])
            dve.wait_ge(l_norm, 16)
            for t in range(2):
                ada_scale(2 + t, mod[:, 0, t * NT:(t + 1) * NT], slice(t * NT, (t + 1) * NT))
            dve.wait_ge(rs_sqrt, 1)
            dve.reciprocal(rstd[:, 0:4], rstd[:, 0:4]).then_inc(rs_done, 1)
            dve.wait_ge(rs_done, 1)
            dve.wait_ge(ada_used, 4)
            dve.engine_nop().then_inc(mod_ready, 1)
            for m in range(4):
                dve.scalar_tensor_tensor(out=x_mix[:, m, :], in0=x_mix[:, m, :], scalar=rstd[:, m:m + 1],
                                         in1=mod[:, 0, :], op0=ALU.mult, op1=ALU.mult).then_inc(hn_step, 1)
                dve.wait_ge(hn_step, m + 1)
                dve.tensor_tensor(x_mix[:, m, :], x_mix[:, m, :], mod[:, 1, :], ALU.add).then_inc(hn_ready, 1)

            def zrow(g):
                return k_end[:, g].rearrange("p d n -> p (d n)")

            dve.wait_ge(l_abias, 32)
            for g in range(4):
                ps = await_job(dve, f"z{g}")
                was_read(dve.tensor_tensor(zrow(g), ps[:, :], a_bias[:, :], ALU.add), f"z{g}")
                after_read(dve, f"z{g}")
                dve.engine_nop().then_inc(z_step, 1)
            for g in range(4):
                dve.scalar_tensor_tensor(out=la[:, g, :], in0=zrow(g), scalar=-1.0, in1=zrow(g),
                                         op0=ALU.mult, op1=ALU.min).then_inc(z_step, 1)
            for g in range(4):
                dve.wait_ge(ln_step, g + 1)
                dve.scalar_tensor_tensor(out=la[:, g, :], in0=zrow(g), scalar=0.0, in1=la[:, g, :],
                                         op0=ALU.min, op1=ALU.subtract).then_inc(la_ready, 1)
            for g in range(4):
                after_read(dve, f"kp{g}")
                after_read(dve, f"qk{g}")
                k_row = qk_rows[:, g, QK:2 * QK] if g < 2 else k_ctx[:, g - 2, :]
                dve.tensor_tensor(k_end[:, g], k_end[:, g], k_row.unsqueeze(1).broadcast_to([P, 2, QK]), ALU.mult)\
                    .then_inc(k_ready, 1)
            for t in range(2):
                ps = await_job(dve, f"qkT{t}")
                after_read(dve, f"bT{t}")
                dve.wait_ge(bx, t + 1)
                for d in range(2):
                    dst = q_dec[:, 2 * d:2 * d + 2, t * P:(t + 1) * P]
                    dve.scalar_tensor_tensor(out=dst, in0=ps[:, 0:256].rearrange("p (a t) -> p a t", a=2),
                                             scalar=DK ** -0.5, in1=dst, op0=ALU.mult, op1=ALU.mult)\
                        .then_inc(qd_ready, 1)
                    dst = k_inv[:, 2 * d:2 * d + 2, t * P:(t + 1) * P]
                    ins = dve.tensor_tensor(dst, ps[:, 256:512].rearrange("p (a t) -> p a t", a=2), dst, ALU.mult)
                    if d == 0:
                        ins.then_inc(qd_ready, 1)
                    else:
                        was_read(ins, f"qkT{t}")
            dve.wait_ge(l_conv, 48)
            for half in range(2):
                ps = await_job(dve, f"x{half}")
                after_read(dve, f"c{half}")
                u = conv_u[:, 2 * half:2 * half + 2, :]
                was_read(dve.tensor_tensor(u, ps[:, :].rearrange("p (f t) -> p f t", f=2), u, ALU.mult), f"x{half}")
            for half in range(2):
                after_read(dve, f"x{half}")
            n_conv = 0
            for f in range(4):
                dve.tensor_scalar(conv_y[:, f, :], conv_u[:, f, :], conv_k[:, 1, f:f + 1], None, ALU.mult)\
                    .then_inc(conv_step, 1)
            for tap, (lo, hi) in ((0, (1, 0)), (2, (0, 1))):
                n_conv += 4
                for f in range(4):
                    dve.wait_ge(conv_step, n_conv - 3 + f)
                    dst = conv_y[:, f, :].rearrange("p (r w) -> p r w", w=GRID_W)[:, :, lo:GRID_W - hi]
                    src = conv_u[:, f, :].rearrange("p (r w) -> p r w", w=GRID_W)[:, :, hi:GRID_W - lo]
                    dve.scalar_tensor_tensor(out=dst, in0=src, scalar=conv_k[:, tap, f:f + 1], in1=dst,
                                             op0=ALU.mult, op1=ALU.add).then_inc(conv_step, 1)
            dve.wait_ge(conv_step, 12)
            for half in range(2):
                ps = await_job(dve, f"b{half}")
                was_read(dve.tensor_tensor(yT[:, 4 + 2 * half:6 + 2 * half, :],
                                           ps[:, :].rearrange("p (f t) -> p f t", f=2),
                                           conv_y[:, 2 * half:2 * half + 2, :], ALU.mult), f"b{half}")
                after_read(dve, f"b{half}")
                dve.engine_nop().then_inc(yconv, 1)
            after_read(dve, "dec")
            for s in range(7):
                for dp in range(4):
                    fwd = dp < 2
                    name = f"kvf{s}" if fwd else f"kvb{s}"
                    ps = await_job(dve, name)
                    kv = ps[:, dp % 2 * DV:(dp % 2 + 1) * DV]
                    if s < 4:
                        ch = s if fwd else 3 - s
                        dst = src = states[:, dp, 0 if fwd else 3, :]
                        dec = decay[:, dp, 4 + ch:5 + ch]
                    else:
                        ch = s - 4 if fwd else 7 - s
                        src = states[:, dp, ch, :]
                        dst = states[:, dp, ch + 1 if fwd else ch - 1, :]
                        dec = decay[:, dp, ch:ch + 1]
                    if s == 0:
                        ins = dve.tensor_copy(dst, kv)
                    else:
                        dve.wait_ge(st_step, 2 * s)
                        after_read(dve, f"kvf{s - 1}")
                        after_read(dve, f"kvb{s - 1}")
                        ins = dve.scalar_tensor_tensor(out=dst, in0=src, scalar=dec, in1=kv,
                                                       op0=ALU.mult, op1=ALU.add)
                    if dp % 2 == 0:
                        ins.then_inc(st_step, 1)
                    else:
                        was_read(ins, name)
            dve.wait_ge(ada_used, 4)
            dve.memset(scores[:, :, :, :, :], 0.0).then_inc(sc_zero, 1)
            dve.wait_ge(sc_zero, 1)
            dve.wait_ge(pool_step, at_step["keep"])
            for t in range(2):
                for odd, name in enumerate((f"sce{t}", f"sco{t}")):
                    ps = await_job(dve, name)
                    was_read(dve.copy_predicated(
                        scores[:, t, odd:HEADS:2].rearrange("p h d t -> p h (d t)"),
                        keep[:, odd:HEADS:2].rearrange("p h d t -> p h (d t)").bitcast(I32),
                        ps[:, 0:2 * P].rearrange("p (h n) -> p h n", h=2)), name)
            ada_add(4, g1_bc[:, 0:NT])
            dve.wait_ge(l_glan, 16)
            for t in range(2):
                after_read(dve, f"oi{t}")
                for odd, name in enumerate((f"oe{t}", f"oo{t}")):
                    ps = await_job(dve, name)
                    dst = o_rows[:, t, :].rearrange("p (h v) -> p h v", h=HEADS)[:, odd:HEADS:2, :]
                    was_read(dve.tensor_tensor(dst, ps[:, 0:2 * DV].rearrange("p (h v) -> p h v", h=2), dst, ALU.add),
                             name)
                after_read(dve, f"oe{t}")
                after_read(dve, f"oo{t}")
                dve.tensor_tensor(o_sq[:, t, :], o_rows[:, t, :], o_rows[:, t, :], ALU.mult).then_inc(o_step, 1)
            for t in range(2):
                dve.wait_ge(o_step, t + 1)
                dve.tensor_reduce(sums[:, 4 + 4 * t:8 + 4 * t], o_sq[:, t, :].rearrange("p (h v) -> p h v", h=HEADS),
                                  AX.X, ALU.add).then_inc(o_sum, 1)
            dve.wait_ge(o_root, 1)
            dve.reciprocal(rstd[:, 4:12], rstd[:, 4:12]).then_inc(o_step, 1)
            for t in range(2):
                dve.wait_ge(r_sig, t + 1)
                dve.tensor_tensor(r_rows[:, t, :], r_rows[:, t, :], o_sq[:, t, :], ALU.mult).then_inc(r_silu, 1)
            dve.wait_ge(o_step, 3)
            for t in range(2):
                view = o_rows[:, t, :].rearrange("p (h v) -> p h v", h=HEADS)
                dve.tensor_tensor(view, view, rstd[:, 4 + 4 * t:8 + 4 * t].unsqueeze(2).broadcast_to([P, HEADS, DV]),
                                  ALU.mult).then_inc(o_step, 1)
                dve.wait_ge(o_step, 4 + 2 * t)
                dve.tensor_tensor(view, view, glan_bc[:, :].unsqueeze(1).broadcast_to([P, HEADS, DV]), ALU.mult)\
                    .then_inc(o_step, 1)
                dve.wait_ge(o_step, 5 + 2 * t)
                dve.wait_ge(r_silu, t + 1)
                dve.tensor_tensor(o_rows[:, t, :], o_rows[:, t, :], r_rows[:, t, :], ALU.mult).then_inc(y_ready, 1)
            ada_add(5, g1_bc[:, NT:2 * NT])
            ada_add(6, mod[:, 1, 0:NT])
            ada_add(7, mod[:, 1, NT:2 * NT])
            dve.wait_ge(l_norm2, 16)
            ada_scale(8, mod[:, 0, 0:NT], slice(0, NT))
            ada_scale(9, mod[:, 0, NT:2 * NT], slice(NT, 2 * NT))
            ada_add(10, g2_bc[:, 0:NT])
            ada_add(11, g2_bc[:, NT:2 * NT])
            dve.wait_ge(l_xres, 16)
            for half in range(2):
                cols = slice(half * NT, (half + 1) * NT)
                for t in range(2):
                    n = 2 * half + t
                    ps = await_job(dve, f"wo{half}{t}")
                    if n:
                        dve.wait_ge(h1_ready, n)
                    was_read(dve.tensor_tensor(scaled[:, :], ps[:, :], g1_bc[:, cols], ALU.mult), f"wo{half}{t}")
                    after_read(dve, f"wo{half}{t}")
                    dve.tensor_tensor(h1[:, t, cols], h1[:, t, cols], scaled[:, :], ALU.add)\
                        .then_inc(h1_ready, 1)
            dve.wait_ge(h_root, 1)
            dve.reciprocal(rstd[:, 12:14], rstd[:, 12:14]).then_inc(h_step, 1)
            dve.wait_ge(h_step, 1)
            for t in range(2):
                dve.scalar_tensor_tensor(out=hn2[:, t, :], in0=h1[:, t, :], scalar=rstd[:, 12 + t:13 + t],
                                         in1=mod[:, 0, :], op0=ALU.mult, op1=ALU.mult).then_inc(h_step, 1)
                dve.wait_ge(h_step, 2 + t)
                dve.tensor_tensor(hn2[:, t, :], hn2[:, t, :], mod[:, 1, :], ALU.add).then_inc(hn2_ready, 1)
            for t in range(2):
                dve.wait_ge(part_a, t + 1)
                dve.tensor_tensor(resid[:, t, :], hn2[:, t, :], hn2_parts[:, t, 0, :], ALU.subtract)\
                    .then_inc(part_r, 1)
            dve.tensor_copy(ident_bf[:, :], ident[:, :]).then_inc(part_r, 1)
            dve.wait_ge(l_router, 32)
            ps = await_job(dve, "logits")
            was_read(dve.tensor_tensor(logit[:, :, :], ps[:, 0:2 * E].rearrange("p (t e) -> p t e", t=2),
                                       r_b[:, :].unsqueeze(1).broadcast_to([P, 2, E]), ALU.add), "logits")
            after_read(dve, "logits")
            for t in range(2):
                dve.max(top[:, t, :], logit[:, t, :]).then_inc(rt, 1)
            dve.wait_ge(rt, 2)
            dve.tensor_tensor(soft[:, :, :], top[:, :, 0:TOPK], top[:, :, 0:1].broadcast_to([P, 2, TOPK]),
                              ALU.subtract).then_inc(rt, 1)
            for t in range(2):
                dve.max_index(top_i[:, t, :], top[:, t, :], logit[:, t, :]).then_inc(rt, 1)
            dve.wait_ge(rt, 5)
            dve.tensor_copy(top_f[:, :, :], top_i[:, :, 0:TOPK]).then_inc(rt, 1)
            dve.wait_ge(rt, 6)
            dve.wait_ge(pool_step, at_step["tables"])
            dve.tensor_tensor(hot[:, :, :, :].rearrange("p t j e -> p (t j) e"),
                              e_no[:, :].unsqueeze(1).broadcast_to([P, 2 * TOPK, E]),
                              top_f[:, :, :].rearrange("p t j -> p (t j)").unsqueeze(2).broadcast_to([P, 2 * TOPK, E]),
                              ALU.is_equal).then_inc(rt, 1)
            dve.wait_ge(rt, 7)
            dve.tensor_reduce(sel[:, :, :], hot[:, :, :, :].rearrange("p t j e -> p t e j"), AX.X, ALU.add)\
                .then_inc(rt_sel, 1)
            dve.wait_ge(rt_exp, 1)
            dve.tensor_reduce(soft_s[:, :], soft[:, :, :], AX.X, ALU.add).then_inc(rt, 1)
            dve.wait_ge(rt, 8)
            dve.reciprocal(soft_r[:, :], soft_s[:, :]).then_inc(rt, 1)
            dve.wait_ge(rt, 9)
            dve.tensor_tensor(w_top[:, :, :], soft[:, :, :], soft_r[:, :].unsqueeze(2).broadcast_to([P, 2, TOPK]),
                              ALU.mult).then_inc(rt, 1)
            dve.wait_ge(rt, 10)
            dve.tensor_tensor(hot_w[:, :, :, :].rearrange("p t j e -> p (t j) e"),
                              hot[:, :, :, :].rearrange("p t j e -> p (t j) e"),
                              w_top[:, :, :].rearrange("p t j -> p (t j)").unsqueeze(2).broadcast_to([P, 2 * TOPK, E]),
                              ALU.mult).then_inc(rt, 1)
            dve.wait_ge(rt, 11)
            dve.tensor_reduce(w_full[:, :, :], hot_w[:, :, :, :].rearrange("p t j e -> p t e j"), AX.X, ALU.add)\
                .then_inc(rt_pos, 1)
            ps = await_job(dve, "rank")
            dve.wait_ge(rt_sel, 1)
            dve.tensor_tensor(pos[:, :, :], ps[:, 0:2 * E].rearrange("p (t e) -> p t e", t=2), sel[:, :, :], ALU.mult)\
                .then_inc(rt_pos, 1)
            dve.tensor_scalar(more[:, :], limits[:, :], ps[0:E, 64:65], None, ALU.is_lt).then_inc(rt, 1)
            dve.wait_ge(rt, 12)
            dve.tensor_reduce(tiles_e[:, :], more[:, :], AX.X, ALU.add).then_inc(rt, 1)
            dve.wait_ge(rt, 13)
            was_read(dve.tensor_scalar(tiles_e[:, :], tiles_e[:, :], 1.0, None, ALU.add), "rank")
            ps = await_job(dve, "start")
            after_read(dve, "rank")
            dve.tensor_copy(begin_e[:, 0:1], ps[0:E, 0:1]).then_inc(rt_own, 1)
            dve.tensor_tensor(begin_e[:, 1:2], ps[0:E, 0:1], tiles_e[:, :], ALU.add).then_inc(rt_own, 1)
            dve.tensor_scalar(begin_e[:, 2:3], ps[0:E, 0:1], float(TOK), None, ALU.mult).then_inc(rt_own, 1)
            dve.tensor_copy(table[0:1, ICOLS:ICOLS + 1], ps[0:1, 1:2]).then_inc(rt_own, 1)
            dve.wait_ge(rt_own, 4)
            dve.tensor_scalar(own[:, :], i_no[0:E, :], begin_e[:, 0:1], None, ALU.is_ge).then_inc(rt_own, 1)
            dve.wait_ge(rt_own, 5)
            dve.scalar_tensor_tensor(out=own[:, :], in0=i_no[0:E, :], scalar=begin_e[:, 1:2], in1=own[:, :],
                                     op0=ALU.is_lt, op1=ALU.mult).then_inc(rt_own, 1)
            ps = await_job(dve, "turn")
            dve.tensor_scalar(routeT[:, 0, :], ps[0:E, 0:SEQ], begin_e[:, 2:3], None, ALU.add).then_inc(rt_T, 1)
            was_read(dve.tensor_copy(routeT[:, 1, :], ps[0:E, SEQ:2 * SEQ]), "turn")
            for t in range(2):
                dve.wait_ge(part_b, t + 1)
                dve.tensor_tensor(hn2_parts[:, t, 2, :], resid[:, t, :], hn2_parts[:, t, 1, :], ALU.subtract)\
                    .then_inc(part_c, 1)
            ps = await_job(dve, "items")
            dve.tensor_copy(table[0:1, 0:ICOLS], ps[0:1, 4 * ICOLS:5 * ICOLS]).then_inc(tab_ready, 1)
            dve.tensor_tensor(item_pos[:, :, :], ps[:, 0:2 * ICOLS].rearrange("p (t i) -> p t i", t=2),
                              i_no64[:, :].unsqueeze(1).broadcast_to([P, 2, ICOLS]), ALU.subtract)\
                .then_inc(it_ready, 1)
            was_read(dve.tensor_copy(item_w[:, :, :], ps[:, 2 * ICOLS:4 * ICOLS].rearrange("p (t i) -> p t i", t=2)),
                     "items")
            dve.wait_ge(it_ready, 1)
            after_read(dve, "items")

            def make_picks(i):
                for t in range(2):
                    col = item_pos[:, t, bass.ds(i, 1)]
                    dve.tensor_scalar(pick[:, t, :], slot_no[:, :, :].rearrange("p a b -> p (a b)"), col, None,
                                      ALU.is_equal).then_inc(pick_ready, 1)
                    dve.tensor_scalar(pick_w[:, t, :], slot_no[:, :, :].rearrange("p a b -> p (a b)"), col,
                                      item_w[:, t, bass.ds(i, 1)], ALU.is_equal, ALU.mult).then_inc(pickw_ready, 1)

            dve.wait_ge(acc_open, 1)
            dve.memset(y_hi[:, :].bitcast(F32), 0.0).then_inc(yhi_s[0], 1)
            dve.memset(y_lo[:, 0:NT].bitcast(F32), 0.0).then_inc(ylo_s[0], 1)
            dve.memset(gu_c[:, 0], 0.0)
            dve.memset(slot_w[:, :], 0.0).then_inc(slot_w_ready, 1)
            dve.memset(put[:, :].bitcast(F32), 0.0).then_inc(put_ready, 1)
            make_picks(0)

            def xs_second():
                dve.tensor_tensor(xs[:, :, TOK:2 * TOK], gather_ps[:, :].rearrange("p (k m) -> p k m", k=KC),
                                  xs[:, :, 0:TOK].bitcast(F32), ALU.subtract).then_inc(xs_ready, 1)

            def y_second(h):
                cols = slice(h * NT, (h + 1) * NT)
                dve.scalar_tensor_tensor(out=y_lo[:, cols], in0=mm[h][:, :], scalar=slot_w[:, 0:1],
                                         in1=y_hi[:, cols].bitcast(F32), op0=ALU.mult, op1=ALU.subtract)\
                    .then_inc(ylo_s[h], 1)

            dve.wait_ge(xs_hi_s, 1)
            xs_second()
            dve.wait_ge(tab_ready, 1)
            n_items = dve.value_load(table[0:1, ICOLS:ICOLS + 1], min_val=1, max_val=ITEMS)
            with dve.Fori(0, ITEMS) as i:
                with dve.If(i < n_items):
                    i4 = dve.snap(i * GU)
                    i12 = dve.snap(i * 2 * SLOTS)
                    def rest(j, pieces=range(2)):
                        for p in pieces:
                            k = WHOLE + p * PIECE
                            dve.wait_ge(hi_done, i12 + 2 * j + p + 1)
                            dve.tensor_tensor(ring_lo[j][:, k:k + PIECE, :], ring[:, j, k:k + PIECE, :],
                                              w_hi[:, j % HI_BUFS, p].bitcast(F32), ALU.subtract).then_inc(lo_done, 1)

                    def clamp(j):
                        dve.wait_ge(folded, i4 + j + 1)
                        b = gu_b[:, j % 2]
                        dve.tensor_tensor(b, fold_ps[:, (j % 2) * 256:(j % 2) * 256 + 256]
                                          .rearrange("p (f t) -> p f t", f=4),
                                          bias_items[:, 4 * j:4 * j + 4, bass.ds(i, 1)].broadcast_to([P, 4, TOK]),
                                          ALU.add).then_inc(biased, 1)
                        dve.wait_ge(biased, i4 + j + 1)
                        dve.tensor_scalar(gu_c[:, j % 2, 0:2, :], b[:, 0:2, :], LIMIT, None, ALU.min)\
                            .then_inc(gate_c, 1)
                        dve.tensor_scalar(gu_c[:, j % 2, 2:4, :], b[:, 2:4, :], LIMIT, -LIMIT, ALU.min, ALU.max)\
                            .then_inc(up_c, 1)

                    def activate(j):
                        dve.wait_ge(sig_done, i4 + j + 1)
                        dve.tensor_tensor(gated[:, j % 2], gu_c[:, j % 2, 0:2, :], sig[:, j % 2], ALU.mult)\
                            .then_inc(gated_s, 1)
                        dve.wait_ge(gated_s, i4 + j + 1)
                        dve.wait_ge(up_c, i4 + j + 1)
                        dve.scalar_tensor_tensor(out=act_full[:, j % 2], in0=gu_c[:, j % 2, 2:4, :], scalar=1.0,
                                                 in1=gated[:, j % 2], op0=ALU.add, op1=ALU.mult).then_inc(actf, 1)
                        dve.wait_ge(actf, i4 + j + 1)
                        st = act_st[:, 2 * j:2 * j + 2, :]
                        dve.tensor_copy(st[:, :, 0:TOK], act_full[:, j % 2]).then_inc(acth, 1)
                        dve.wait_ge(acth, i4 + j + 1)
                        dve.tensor_tensor(st[:, :, TOK:2 * TOK], act_full[:, j % 2], st[:, :, 0:TOK].bitcast(F32),
                                          ALU.subtract).then_inc(act_ready, 1)

                    rest(0)
                    rest(1)
                    dve.wait_ge(yhi_s[1], i + 1)
                    y_second(1)
                    rest(2)
                    rest(3)
                    clamp(0)
                    activate(0)
                    rest(4)
                    clamp(1)
                    activate(1)
                    dve.wait_ge(turned, i + 1)
                    dve.tensor_copy(put[:, :], gather_ps[:, 0:SEQ]).then_inc(put_ready, 1)
                    dve.tensor_copy(slot_w[:, :], gather_ps[:, SEQ:SEQ + 1]).then_inc(slot_w_ready, 1)
                    clamp(2)
                    activate(2)
                    make_picks(i + 1)
                    rest(5, (0,))
                    clamp(3)
                    activate(3)
                    rest(5, (1,))
                    dve.wait_ge(xs_hi_s, i + 2)
                    xs_second()
                    dve.wait_ge(slot_w_ready, i + 2)
                    dve.wait_ge(yhi_s[0], i + 2)
                    y_second(0)
            dve.wait_ge(yhi_s[1], n_items + 1)
            y_second(1)
            dve.wait_ge(scattered, n_items + 1)
            dve.wait_ge(l_fin, 16)
            for t in range(2):
                for h in range(2):
                    cols = slice(h * NT, (h + 1) * NT)
                    dve.tensor_tensor(fin_y[:, t, cols], acc[2 * t + h][:, :], g2_bc[:, cols], ALU.mult)\
                        .then_inc(f_step, 1)
                dve.wait_ge(f_step, 4 * t + 2)
                for h in range(2):
                    cols = slice(h * NT, (h + 1) * NT)
                    dve.tensor_tensor(fin_y[:, t, cols], fin_y[:, t, cols], h1[:, t, cols], ALU.add)\
                        .then_inc(f_step, 1)
            dve.wait_ge(f_root, 1)
            dve.reciprocal(rstd_f[:, 0:2], rstd_f[:, 0:2]).then_inc(f_step, 1)
            dve.wait_ge(f_step, 9)
            for t in range(2):
                dve.scalar_tensor_tensor(out=fin_y[:, t, :], in0=fin_y[:, t, :], scalar=rstd_f[:, t:t + 1],
                                         in1=fin_n[:, :], op0=ALU.mult, op1=ALU.mult).then_inc(f_step, 1)

        @block.tensor
        def _(pe):
            def tile_landed(t):
                pe.wait_ge(landed[head_slot(t)], 16 * (head_nth(t) + 1))

            def product(ps, lhs, t, cols=slice(0, NT)):
                for k in range(KC):
                    ins = pe.matmul(ps, lhs(k), ring[:, head_slot(t), k, cols], start=(k == 0), stop=(k == KC - 1))
                return ins

            pe.wait_ge(pool_step, at_step["ident"])
            pe.wait_ge(c_silud, 1)
            ps = await_bank(pe, "cT")
            filled(pe.transpose(ps[:, 0:2 * KC], c_rows[:, :], ident[0:2 * KC, 0:2 * KC]), "cT")
            after_read(pe, "cT")
            pe.wait_ge(c_ready, 1)

            def ada(a, t, lhs):
                tile_landed(t)
                ps = await_bank(pe, f"ada{a}")
                filled(product(ps[:, :], lhs, t), f"ada{a}")

            for a in range(4):
                ada(a, a, lambda k: c_mix[:, k].rearrange("p a b -> p (a b)"))
            for m in range(4):
                pe.wait_ge(hn_ready, m + 1)
                for half in range(2):
                    ps = await_bank(pe, f"hnT{m}{half}")
                    for k in range(4):
                        ins = pe.transpose(ps[:, k * P:(k + 1) * P], x_mix[:, m, (4 * half + k) * P:(4 * half + k + 1) * P],
                                           ident[:, :])
                    filled(ins, f"hnT{m}{half}")
            after_read(pe, "hnT30")
            after_read(pe, "hnT31")
            pe.wait_ge(l_aa, 16)
            ps = await_bank(pe, "aa")
            for s in range(2):
                for k in range(KC):
                    ins = pe.matmul(ps[0:2 * RANK, s * SEQ:(s + 1) * SEQ], w_aa[:, k, :], hnT[:, s, k, :],
                                    start=(k == 0), stop=(k == KC - 1))
            filled(ins, "aa")
            tile_landed(4)
            for g in range(4):
                ps = await_bank(pe, f"qk{g}")
                if g < 2:
                    filled(product(ps[:, :], tok(g), 4), f"qk{g}")
                else:
                    filled(product(ps[:, 0:QK], tok(g), 4, slice(QK, 2 * QK)), f"qk{g}")
            after_read(pe, "aa")
            pe.wait_ge(l_up, 32)
            for g in range(4):
                ps = await_bank(pe, f"z{g}")
                filled(pe.matmul(ps[:, :], aT[:, g * P:(g + 1) * P], up_blk[:, :], start=True, stop=True), f"z{g}")
            tile_landed(5)
            for g in range(4):
                ps = await_bank(pe, f"v{g}")
                filled(product(ps[:, :], tok(g), 5), f"v{g}")
            pe.wait_ge(pool_step, at_step["scan"])
            for g in range(4):
                pe.wait_ge(la_ready, g + 1)
                ps = await_bank(pe, f"kp{g}")
                for d in range(2):
                    ins = pe.matmul(ps[:, d * QK:(d + 1) * QK], beyond[:, d, :], la[:, g, d * QK:(d + 1) * QK],
                                    start=True, stop=True)
                filled(ins, f"kp{g}")
            ps = await_bank(pe, "dec")
            for g in range(4):
                for dp in range(4):
                    col = 8 * g + 2 * dp
                    ins = pe.matmul(ps[:, col:col + 2], la[:, g, dp * P:(dp + 1) * P], in_chunk[:, :],
                                    start=True, stop=True)
            filled(ins, "dec")
            for t in range(2):
                ps = await_bank(pe, f"bT{t}")
                for dp in range(4):
                    ins = pe.matmul(ps[:, dp * P:(dp + 1) * P], la[:, t, dp * P:(dp + 1) * P], up_to[:, dp // 2, :],
                                    start=True, stop=True)
                filled(ins, f"bT{t}")
            tile_landed(6)
            for t in range(2):
                ps = await_bank(pe, f"r{t}")
                filled(product(ps[:, :], tok(t), 6), f"r{t}")
            for t in range(2):
                ps = await_bank(pe, f"qkT{t}")
                for a in range(4):
                    ins = pe.transpose(ps[:, a * P:(a + 1) * P], qk_rows[:, t, a * P:(a + 1) * P], ident[:, :])
                filled(ins, f"qkT{t}")
            for n, what in enumerate("cxb"):
                t = 7 + n
                tile_landed(t)
                for half in range(2):
                    ps = await_bank(pe, f"{what}{half}")
                    for f in range(2):
                        for k in range(KC):
                            ins = pe.matmul(ps[:, f * SEQ:(f + 1) * SEQ],
                                            ring[:, head_slot(t), k, (2 * half + f) * P:(2 * half + f + 1) * P],
                                            hnT[:, 0, k, :], start=(k == 0), stop=(k == KC - 1))
                    filled(ins, f"{what}{half}")
            pe.wait_ge(k_ready, 4)
            after_read(pe, "v3")
            after_read(pe, "v2")
            for s in range(7):
                for dp in range(4):
                    name = f"kvf{s}" if dp < 2 else f"kvb{s}"
                    ps = await_bank(pe, name) if dp % 2 == 0 else bank[JOBS[name][0]]
                    step = s if s < 4 else s - 4
                    ch = step if dp < 2 else 3 - step
                    g = (2 if s < 4 else 0) + ch // 2
                    rows = slice((ch % 2) * CH, (ch % 2) * CH + CH)
                    for hh in range(2):
                        h = 2 * (dp % 2) + hh
                        ins = pe.matmul(ps[hh * DK:(hh + 1) * DK, dp % 2 * DV:(dp % 2 + 1) * DV],
                                        k_end[rows, g, dp // 2, h * DK:(h + 1) * DK],
                                        v_rows[rows, g, h * DV:(h + 1) * DV], start=True, stop=True,
                                        skip_group_check=True)
                    if dp % 2:
                        filled(ins, name)
            after_read(pe, "qkT1")
            after_read(pe, "qkT0")
            pe.wait_ge(qd_ready, 6)
            for t in range(2):
                for odd, name in enumerate((f"sce{t}", f"sco{t}")):
                    ps = await_bank(pe, name)
                    rows = slice(odd * DK, (odd + 1) * DK)
                    for cc, h, d in [(cc, h, d) for cc in range(2) for h in (odd, odd + 2) for d in range(2)]:
                            toks = slice(t * P + cc * CH, t * P + cc * CH + CH)
                            col = (2 * (h // 2) + d) * CH
                            ins = pe.matmul(ps[cc * CH:(cc + 1) * CH, col:col + CH],
                                            k_inv[rows, 2 * d + h // 2, toks], q_dec[rows, 2 * d + h // 2, toks],
                                            start=True, stop=True, skip_group_check=True)
                    filled(ins, name)
            ada(4, 10, lambda k: c_all[:, k, :])
            after_read(pe, "kvf6")
            after_read(pe, "kvb6")
            for t in range(2):
                after_read(pe, f"sce{t}")
                after_read(pe, f"sco{t}")
                within = await_bank(pe, f"oi{t}")
                for cc in range(2):
                    rows = slice(cc * CH, (cc + 1) * CH)
                    for h in range(HEADS):
                        for d in range(2):
                            ins = pe.matmul(within[rows, h * DV:(h + 1) * DV], scores[rows, t, h, d, :],
                                            v_rows[rows, t, h * DV:(h + 1) * DV], start=(d == 0), stop=(d == 1),
                                            skip_group_check=True)
                filled(ins, f"oi{t}")
                for odd, name in enumerate((f"oe{t}", f"oo{t}")):
                    before = await_bank(pe, name)
                    rows = slice(odd * DK, (odd + 1) * DK)
                    for cc in range(2):
                        toks = slice(t * P + cc * CH, t * P + cc * CH + CH)
                        for hp in range(2):
                            for d in range(2):
                                ins = pe.matmul(before[cc * CH:(cc + 1) * CH, hp * DV:(hp + 1) * DV],
                                                q_dec[rows, 2 * d + hp, toks], states[rows, 2 * d + hp, 2 * t + cc, :],
                                                start=(d == 0), stop=(d == 1), skip_group_check=True)
                    filled(ins, name)
            for a in range(5, 9):
                ada(a, 6 + a, lambda k: c_all[:, k, :])
            for t in range(2):
                pe.wait_ge(y_ready, t + 1)
                ps = await_bank(pe, f"yT{t}")
                for f in range(4):
                    ins = pe.transpose(ps[:, f * P:(f + 1) * P], o_rows[:, t, f * P:(f + 1) * P], ident[:, :])
                filled(ins, f"yT{t}")
            for a in range(9, 12):
                ada(a, 6 + a, lambda k: c_all[:, k, :])
            after_read(pe, "yT0")
            after_read(pe, "yT1")
            pe.wait_ge(yconv, 2)
            for half in range(2):
                tile_landed(18 + half)
                for t in range(2):
                    ps = await_bank(pe, f"wo{half}{t}")
                    filled(product(ps[:, :], lambda k: yT[:, k, t * P:(t + 1) * P], 18 + half), f"wo{half}{t}")
            for t in range(2):
                pe.wait_ge(hn2_ready, t + 1)
                for half in range(2):
                    ps = await_bank(pe, f"h2T{t}{half}")
                    for k in range(4):
                        ins = pe.transpose(ps[:, k * P:(k + 1) * P], hn2[:, t, (4 * half + k) * P:(4 * half + k + 1) * P],
                                           ident[:, :])
                    filled(ins, f"h2T{t}{half}")
            for t in range(2):
                for half in range(2):
                    after_read(pe, f"h2T{t}{half}")
            pe.wait_ge(l_router, 32)
            ps = await_bank(pe, "logits")
            for t in range(2):
                for k in range(KC):
                    ins = pe.matmul(ps[:, t * E:(t + 1) * E], h2T[:, k, t * P:(t + 1) * P], r_w[:, k, :],
                                    start=(k == 0), stop=(k == KC - 1))
            filled(ins, "logits")
            pe.wait_ge(rt_sel, 1)
            pe.wait_ge(pool_step, at_step["tables"])
            ps = await_bank(pe, "rank")
            pe.matmul(ps[:, 0:E], tri[:, :], sel[:, 0, :], start=True, stop=True)
            pe.matmul(ps[:, E:2 * E], tri[:, :], sel[:, 1, :], start=True, stop=False)
            pe.matmul(ps[:, E:2 * E], ones[:, :], sel[:, 0, :], start=False, stop=True)
            for t in range(2):
                ins = pe.matmul(ps[0:E, 64:65], sel[:, t, :], ones[:, 0:1], start=(t == 0), stop=(t == 1))
            filled(ins, "rank")
            pe.wait_ge(rt_pos, 2)
            ps = await_bank(pe, "turn")
            for n, src in enumerate((pos, w_full)):
                for t in range(2):
                    ins = pe.transpose(ps[0:E, (2 * n + t) * P:(2 * n + t + 1) * P], src[:, t, :], ident[:, :])
            filled(ins, "turn")
            after_read(pe, "rank")
            ps = await_bank(pe, "start")
            pe.matmul(ps[0:E, 0:1], below[:, :], tiles_e[:, :], start=True, stop=True)
            filled(pe.matmul(ps[0:1, 1:2], tiles_e[:, :], ones[0:E, 0:1], start=True, stop=True), "start")
            pe.wait_ge(rt_own, 6)
            pe.wait_ge(rt_T, 1)
            after_read(pe, "turn")
            ps = await_bank(pe, "items")
            for n in range(2):
                for t in range(2):
                    col = (2 * n + t) * ICOLS
                    pe.matmul(ps[:, col:col + ICOLS], routeT[:, n, t * P:(t + 1) * P], own[:, :], start=True, stop=True)
            filled(pe.matmul(ps[0:1, 4 * ICOLS:5 * ICOLS], e_col[:, :], own[:, :], start=True, stop=True), "items")
            pe.wait_ge(l_bgu, 16)
            for half in range(2):
                ps = await_bank(pe, f"bias{half}")
                for n in range(8):
                    j, part = (8 * half + n) // 4, (8 * half + n) % 4
                    first = 2 * P * (2 * j + part % 2) + part // 2
                    ins = pe.matmul(ps[:, n * ICOLS:(n + 1) * ICOLS], bgu_rows[:, first:first + 2 * P - 1:2], own[:, :],
                                    start=True, stop=True)
                filled(ins, f"bias{half}")
            pe.wait_ge(l_bdn, 16)
            for name in ("rank", "turn", "items", "bias0", "ada10", "ada11"):
                after_read(pe, name)
            for t in range(2):
                for h in range(2):
                    ins = pe.matmul(acc[2 * t + h][:, :], routeT[:, 1, t * P:(t + 1) * P],
                                    bdn_rows[:, h * NT:(h + 1) * NT], start=True, stop=False, skip_group_check=True)
            ins.then_inc(acc_open, 1)

            def gather():
                for k in range(KC):
                    for t in range(2):
                        for part in range(3):
                            ins = pe.matmul(gather_ps[:, k * TOK:(k + 1) * TOK], hn2_parts[:, t, part, k * P:(k + 1) * P],
                                            pick[:, t, 0:TOK], start=(t == 0 and part == 0),
                                            stop=(t == 1 and part == 2))
                ins.then_inc(gathered, 1)

            def scatter(last):
                for t in range(2):
                    for h in range(2):
                        for n, src in enumerate((y_hi, y_lo)):
                            ins = pe.matmul(acc[2 * t + h][:, :], put[:, t * P:(t + 1) * P],
                                            src[:, h * NT:(h + 1) * NT], start=False, stop=(last and n == 1),
                                            skip_group_check=True)
                ins.then_inc(scattered, 1)

            pe.wait_ge(pick_ready, 2)
            pe.wait_ge(part_c, 2)
            pe.wait_ge(part_r, 3)
            gather()
            pe.wait_ge(tab_ready, 1)
            after_read(pe, "bias1")
            for j in range(SLOTS):
                pe.nop().then_inc(used[j], 1)
            n_items = pe.value_load(table[0:1, ICOLS:ICOLS + 1], min_val=1, max_val=ITEMS)
            with pe.Fori(0, ITEMS) as i:
                with pe.If(i < n_items):
                    i4 = pe.snap(i * GU)
                    i12 = pe.snap(i * 2 * SLOTS)
                    def whole(j, lhs, chunks):
                        for k in chunks:
                            pe.matmul(mm[j % 2][:, :], lhs[:, k, :].bitcast(F32), ring[:, j, k, :],
                                      start=(k == 0), stop=False)

                    def split(j, lhs):
                        for p in range(2):
                            pe.wait_ge(lo_done, i12 + 2 * j + p + 1)
                            if j == 4:
                                pe.wait_ge(act_ready, i4 + 3 + p)
                            for s in range(PIECE):
                                k = WHOLE + p * PIECE + s
                                for n, half in enumerate((w_hi[:, j % HI_BUFS, p, s, :], ring_lo[j][:, k, :])):
                                    ins = pe.matmul(mm[j % 2][:, :], lhs[:, k, :], half,
                                                    start=False, stop=(k == KC - 1 and n == 1))
                        ins.then_inc(used[j], 1)

                    def gate_up(j):
                        pe.wait_ge(landed[j], 16 * (i + HEAD_USES[j] + 1))
                        if j < 2:
                            pe.wait_ge(ylo_s[j], i + 1)
                        else:
                            pe.wait_ge(rows_out, i4 + j - 1)
                        whole(j, xs, range(WHOLE))
                        split(j, xs)

                    def fold_rows(j):
                        pe.wait_ge(rows_out, i4 + j + 1)
                        if j:
                            pe.wait_ge(biased, i4 + j)
                        for part in range(4):
                            first = 2 * P * (2 * j + part % 2) + part // 2
                            col = (j % 2) * 256 + part * TOK
                            ins = pe.matmul(fold_ps[:, col:col + TOK], gu_rows[:, first:first + 2 * P - 1:2],
                                            fold[:, :], start=True, stop=True)
                        ins.then_inc(folded, 1)

                    pe.wait_ge(xs_ready, i + 1)
                    gate_up(0)
                    gate_up(1)
                    fold_rows(0)
                    gate_up(2)
                    fold_rows(1)
                    pe.wait_ge(put_ready, i + 1)
                    pe.wait_ge(ylo_s[0], i + 1)
                    pe.wait_ge(ylo_s[1], i + 1)
                    scatter(False)
                    pe.wait_ge(pick_ready, 2 * i + 2)
                    pe.wait_ge(pickw_ready, 2 * i + 2)
                    for t in range(2):
                        pe.matmul(gather_ps[:, t * P:(t + 1) * P], pick[:, t, :], ident_bf[:, :],
                                  start=True, stop=True)
                    for t in range(2):
                        ins = pe.matmul(gather_ps[:, SEQ:SEQ + 1], pick_w[:, t, :], ones[:, 0:1],
                                        start=(t == 0), stop=(t == 1))
                    ins.then_inc(turned, 1)
                    fold_rows(2)
                    gate_up(3)
                    pe.wait_ge(landed[4], 16 * (i + HEAD_USES[4] + 1))
                    pe.wait_ge(act_ready, i4 + 1)
                    whole(4, act_st, (0,))
                    fold_rows(3)
                    whole(4, act_st, range(1, WHOLE))
                    pe.wait_ge(pick_ready, 2 * i + 4)
                    pe.wait_ge(put_ready, i + 2)
                    pe.wait_ge(slot_w_ready, i + 2)
                    gather()
                    split(4, act_st)
                    pe.wait_ge(landed[5], 16 * (i + HEAD_USES[5] + 1))
                    whole(5, act_st, range(WHOLE))
                    split(5, act_st)
            pe.wait_ge(put_ready, n_items + 1)
            pe.wait_ge(ylo_s[0], n_items + 1)
            pe.wait_ge(ylo_s[1], n_items + 1)
            scatter(True)


_INS = ['x', 'c', 'ctx', 'c_ctx', 'w_ada', 'b_ada', 'norm1_w', 'w_in', 'a_up_f', 'a_bias_f', 'a_up_b', 'a_bias_b',
        'gla_norm_w', 'conv_w', 'w_out', 'norm2_w', 'router_w', 'router_b', 'w_gu', 'b_gu', 'w_dn', 'b_dn',
        'final_norm_w']
_OUTS = [((1, 256, 1024), 'float32')]


def kernel(**inputs):
    import numpy as _np
    import concourse.bacc as _bacc
    from concourse import mybir as _mybir
    from concourse.bass_utils import run_bass_kernel_spmd as _run

    nc = _bacc.Bacc("TRN2", target_bir_lowering=False, num_devices=1)
    arrays, args = {}, []
    for name in _INS:
        a = _np.ascontiguousarray(inputs[name])
        arrays[f"in_{name}_dram"] = a
        args.append(nc.dram_tensor(f"in_{name}_dram", a.shape, _mybir.dt.from_np(a.dtype), kind="ExternalInput").ap())
    for i, (shape, dtype) in enumerate(_OUTS):
        dt = _mybir.dt.from_np(_np.dtype(dtype))
        args.append(nc.dram_tensor(f"out_{i}_dram", shape, dt, kind="ExternalOutput").ap())
    hybrid_layer(nc, *args)
    r = _run(nc, [arrays], core_ids=[0])
    got = tuple(r.results[0][f"out_{i}_dram"] for i in range(len(_OUTS)))
    return got[0]
```

```python
from contextlib import ExitStack

import concourse.bass as bass
from concourse import mybir

F32 = mybir.dt.float32
F32R = mybir.dt.float32r
BF16 = mybir.dt.bfloat16
I32 = mybir.dt.int32
U32 = mybir.dt.uint32
ALU = mybir.AluOpType
ACT = mybir.ActivationFunctionType
AX = mybir.AxisListType

P = 128
D = 1024
KC = D // P
NT = 512
SEQ = 256
GRID_W = 64
HEADS, DK, DV = 4, 64, 128
QK = HEADS * DK
GLA_W = HEADS * DV
CONV_W = D - GLA_W
RANK = 16
CH = 64
NCH = SEQ // CH
E = 32
TOPK = 4
FF = D
LIMIT, ALPHA, EPS = 7.0, 1.702, 1e-6
GATE_NORM = 16.0

Q0, V0, R0 = 0, 2 * QK, 2 * QK + GLA_W
AF0 = R0 + GLA_W
B0 = AF0 + 2 * RANK
C0, X0 = B0 + CONV_W, B0 + 2 * CONV_W

TOK = 64
ITEMS = E + (SEQ * TOPK - E) // TOK
GROUP = 4
GROUPS = -(-ITEMS // GROUP)
ICOLS = GROUPS * GROUP + 1
SLOTS = 6
GU, DN = 4, 2
SPLIT = 6
PIECE = SPLIT // 2
HI_BUFS = 3
WHOLE = KC - SPLIT

ADA = [("ada", NT * n) for n in range(12)]
HEAD_TILES = (ADA[0:5] + [("in", Q0)] + ADA[5:7] + [("in", V0)] + ADA[7:9] + [("in", R0), ("in", C0), ADA[9]]
              + [("in", X0), ("in", B0), ADA[10], ("out", 0), ("out", NT), ADA[11]])
NHEAD = len(HEAD_TILES)
FIRST_SLOT = (-NHEAD) % SLOTS


def head_slot(t):
    return (t + FIRST_SLOT) % SLOTS


def head_nth(t):
    return sum(head_slot(u) == head_slot(t) for u in range(t))


LAST_JOB = [f"ada{col // NT}" if what == "ada" else
            {("in", Q0): "qk3", ("in", V0): "v3", ("in", R0): "r1", ("in", C0): "c1", ("in", X0): "x1",
             ("in", B0): "b1", ("out", 0): "wo01", ("out", NT): "wo11"}[what, col] for what, col in HEAD_TILES]
HEAD_USES = [sum(head_slot(t) == j for t in range(NHEAD)) for j in range(SLOTS)]

JOBS = {}
BANK_USES = [0] * 8


def add_job(name, bank):
    JOBS[name] = (bank, BANK_USES[bank])
    BANK_USES[bank] += 1


def plan_jobs():
    JOBS.clear()
    BANK_USES[:] = [0] * 8
    turn = {}

    def job(name, banks):
        n = turn.get(banks, 0)
        turn[banks] = n + 1
        add_job(name, banks[n % len(banks)])

    job("cT", (7,))
    for t in range(5):
        job(f"ada{t}", (0, 1))
    for m in range(4):
        for half in range(2):
            job(f"hnT{m}{half}", (2, 3))
    job("aa", (7,))
    for g in range(4):
        job(f"qk{g}", (4, 5, 6))
    for a in (5, 6):
        job(f"ada{a}", (1, 0))
    for g in range(4):
        job(f"z{g}", (2, 3))
    for g in range(4):
        job(f"v{g}", (4, 5, 6))
    for a in (7, 8):
        job(f"ada{a}", (1, 0))
    for g in range(4):
        job(f"kp{g}", (2, 3))
    job("dec", (7,))
    for t in range(2):
        job(f"bT{t}", (2, 3))
    for t in range(2):
        job(f"r{t}", (4, 5, 6))
    for t in range(2):
        job(f"qkT{t}", (2, 3))
    for what in "cxb":
        for half in range(2):
            job(f"{what}{half}", (4, 5, 6))
            s = 2 * "cxb".index(what) + half
            job(f"kvf{s}", (2, 7))
            job(f"kvb{s}", (3, 6))
        if what == "c":
            job("ada9", (1, 0))
    job("kvf6", (2, 7))
    job("kvb6", (3, 6))
    for t in range(2):
        job(f"sce{t}", (2, 7))
        job(f"sco{t}", (3, 6))
    for t in range(2):
        job(f"oi{t}", (4, 5))
        job(f"oe{t}", (2, 7))
        job(f"oo{t}", (3, 6))
    job("ada10", (1, 0))
    for t in range(2):
        job(f"yT{t}", (2, 3))
    for half in range(2):
        for t in range(2):
            job(f"wo{half}{t}", (4, 5, 6))
    job("ada11", (1, 0))
    for t in range(2):
        for half in range(2):
            job(f"h2T{t}{half}", (2, 3))
    job("logits", (7,))
    job("rank", (0,))
    job("turn", (1,))
    job("start", (7,))
    job("items", (2,))
    job("bias0", (3,))
    job("bias1", (6,))


def hybrid_layer(nc, x, c, ctx_tok, c_ctx, w_ada, b_ada, norm1_w, w_in, a_up_f, a_bias_f, a_up_b, a_bias_b,
                 gla_norm_w, conv_w, w_out, norm2_w, router_w, router_b, w_gu, b_gu, w_dn, b_dn,
                 final_norm_w, out):
    plan_jobs()
    with ExitStack() as stack:
        base = (nc.sbuf_base + 63) // 64 * 64
        cursor = [base]

        def at(name, shape, dt=F32, offset=None):
            n = 4
            for s in shape[1:]:
                n *= s
            if dt == BF16:
                n //= 2
            n = (n + 31) // 32 * 32
            o = cursor[0] if offset is None else offset
            if offset is None:
                cursor[0] += n
            return nc.alloc_sbuf_tensor_at(name, shape, dt, offset=o)

        ring = at("ring", [P, SLOTS, KC, NT])
        ring_lo = [at(f"ring_lo{j}", [P, KC, NT], F32R, offset=base + 4 * KC * NT * j) for j in range(SLOTS)]
        hn2_at = cursor[0]
        hn2 = at("hn2", [P, 2, D])
        h1_at = cursor[0]
        h1 = at("h1", [P, 2, D])
        g2_at = cursor[0]
        g2_bc = at("g2_bc", [P, D])
        bias_items = at("bias_items", [P, 16, ICOLS])
        item_pos = at("item_pos", [P, 2, ICOLS])
        item_w = at("item_w", [P, 2, ICOLS])
        ident = at("ident", [P, P])
        slot_no = at("slot_no", [P, 2, TOK])
        ones = at("ones", [P, P])
        fold = at("fold", [P, TOK])
        table = at("table", [1, ICOLS + 1], I32)
        eps_col = at("eps_col", [P, 1])
        one_col = at("one_col", [P, 1])
        loop_at = cursor[0]
        xs = at("xs", [P, KC, 2 * TOK], F32R)
        gu_rows = at("gu_rows", [P, GU * NT])
        act_st = at("act_st", [P, KC, 2 * TOK], F32R)
        parts_at = cursor[0]
        hn2_parts = at("hn2_parts", [P, 2, 3, D], BF16)
        w_hi = at("w_hi", [P, HI_BUFS, 2, PIECE, NT], F32R)
        ident_bf = at("ident_bf", [P, P], BF16)
        y_hi = at("y_hi", [P, D], F32R)
        y_lo = at("y_lo", [P, D], F32R)
        pick = at("pick", [P, 2, 2 * TOK], BF16)
        pick_w = at("pick_w", [P, 2, 2 * TOK])
        put = at("put", [P, SEQ], F32R)
        slot_w = at("slot_w", [P, 1])
        gu_b = at("gu_b", [P, 2, 4, TOK])
        gu_c = at("gu_c", [P, 2, 4, TOK])
        sig = at("sig", [P, 2, 2, TOK])
        gated = at("gated", [P, 2, 2, TOK])
        act_at = cursor[0]
        act_full = at("act_full", [P, 2, 2, TOK])
        zeros = at("zeros", [P, P], BF16, offset=act_at)
        assert cursor[0] <= nc.sbuf_usable_end, (cursor[0], nc.sbuf_usable_end)

        loop_end = cursor[0]
        cursor[0] = loop_at
        hnT_at = cursor[0]
        hnT = at("hnT", [P, 2, KC, SEQ])
        st_at = cursor[0]
        assert parts_at == st_at
        states = at("states", [P, 4, NCH, DV])
        mod = at("mod", [P, 2, D])
        resid = at("resid", [P, 2, D], offset=cursor[0])
        g1_bc = at("g1_bc", [P, D])
        norm_bc = at("norm_bc", [P, D])
        bias_at = cursor[0]
        ada_bias = at("ada_bias", [P, 2, NT])
        v_at = cursor[0]
        v_rows = at("v_rows", [P, 4, GLA_W])
        k_ctx = at("k_ctx", [P, 2, QK])
        yT = at("yT", [P, KC, SEQ])
        gate_at = cursor[0]
        aT = at("aT", [2 * RANK, 2 * SEQ])
        up_blk = at("up_blk", [2 * RANK, 2 * QK])
        a_bias = at("a_bias", [P, 2 * QK])
        la_at = cursor[0]
        la = at("la", [P, 4, 2 * QK])
        cmix_at = cursor[0]
        c_mix = at("c_mix", [P, KC, 2, 64])
        call_at = cursor[0]
        c_all = at("c_all", [P, KC, P])
        tri = at("tri", [P, P])
        up_to = at("up_to", [P, 2, P], offset=g2_at)
        beyond = at("beyond", [P, 2, P], offset=g2_at + 1024)
        in_chunk = at("in_chunk", [P, 2])
        glan_bc = at("glan_bc", [P, DV], offset=g2_at + 2048)
        w_aa = at("w_aa", [P, KC, 2 * RANK], offset=g2_at + 2560)
        conv_k = at("conv_k", [P, 3, CONV_W // P])
        c_rows = at("c_rows", [2 * KC, P])
        c_sig = at("c_sig", [2 * KC, P])
        sums = at("sums", [P, 16])
        rstd = at("rstd", [P, 16])
        decay = at("decay", [P, 4, 2 * NCH])
        assert cursor[0] <= nc.sbuf_usable_end, (cursor[0], nc.sbuf_usable_end)
        x_mix = at("x_mix", [P, 4, D], offset=hn2_at)
        k_end = at("k_end", [P, 4, 2, QK], offset=hn2_at)
        ada_bias4 = at("ada_bias4", [P, 4, NT], offset=v_at)
        r_rows = at("r_rows", [P, 2, GLA_W], offset=h1_at)
        qk_rows = at("qk_rows", [P, 2, 2 * QK], offset=h1_at + 4096)
        q_dec = at("q_dec", [P, 4, SEQ], offset=la_at)
        k_inv = at("k_inv", [P, 4, SEQ], offset=la_at + 4096)
        scores = at("scores", [P, 2, HEADS, 2, CH], offset=cmix_at)
        conv_u = at("conv_u", [P, 4, SEQ], offset=hnT_at + 8192)
        conv_y = at("conv_y", [P, 4, SEQ], offset=hnT_at + 12288)
        o_rows = at("o_rows", [P, 2, GLA_W], offset=hnT_at + 8192)
        o_sq = at("o_sq", [P, 2, GLA_W], offset=hnT_at + 12288)
        keep = at("keep", [P, HEADS, 2, CH], offset=gate_at)
        scaled = at("scaled", [P, GLA_W], offset=gate_at + 2048)
        h2T = at("h2T", [P, KC, SEQ], offset=hnT_at)
        bgu_rows = at("bgu_rows", [E, 2 * FF], offset=hnT_at + 8192)
        bdn_rows = at("bdn_rows", [E, D], offset=hn2_at)
        assert call_at + 2048 >= loop_end
        r_w = at("r_w", [P, KC, E], offset=cmix_at)
        rt_at = cmix_at + 1024
        r_b = at("r_b", [P, E], offset=rt_at)
        logit = at("logit", [P, 2, E], offset=rt_at + 128)
        top = at("top", [P, 2, 8], offset=rt_at + 384)
        top_i = at("top_i", [P, 2, 8], U32, offset=rt_at + 448)
        top_f = at("top_f", [P, 2, TOPK], offset=rt_at + 512)
        soft = at("soft", [P, 2, TOPK], offset=rt_at + 544)
        soft_s = at("soft_s", [P, 2], offset=rt_at + 576)
        soft_r = at("soft_r", [P, 2], offset=rt_at + 608)
        w_top = at("w_top", [P, 2, TOPK], offset=rt_at + 640)
        sel = at("sel", [P, 2, E], offset=rt_at + 672)
        w_full = at("w_full", [P, 2, E], offset=rt_at + 928)
        pos = at("pos", [P, 2, E], offset=rt_at + 1184)
        e_no = at("e_no", [P, E], offset=rt_at + 1440)
        i_no = at("i_no", [P, ICOLS], offset=rt_at + 1568)
        i_no64 = at("i_no64", [P, ICOLS], offset=rt_at + 1792)
        limits = at("limits", [E, 3], offset=rt_at + 2016)
        more = at("more", [E, 3], offset=rt_at + 2048)
        tiles_e = at("tiles_e", [E, 1], offset=rt_at + 2080)
        begin_e = at("begin_e", [E, 4], offset=rt_at + 2112)
        e_col = at("e_col", [E, 1], offset=rt_at + 2144)
        below = at("below", [E, E], offset=rt_at + 2176)
        own = at("own", [E, ICOLS], offset=rt_at + 2304)
        hot = at("hot", [P, 2, TOPK, E], offset=bias_at)
        hot_w = at("hot_w", [P, 2, TOPK, E], offset=bias_at + 1024)
        routeT = at("routeT", [E, 2, SEQ], offset=call_at + 2048)
        fin_n = at("fin_n", [P, D], offset=base)
        fin_y = at("fin_y", [P, 2, D], offset=base + 4096)
        fin_sq = at("fin_sq", [P, 2, D], offset=base + 12288)

        sums_f = at("sums_f", [P, 2], offset=base + 20480)
        rstd_f = at("rstd_f", [P, 2], offset=base + 20512)

        bank = [stack.enter_context(nc.psum_tensor(f"bank{b}", [P, NT], F32)) for b in range(8)]
        acc = bank[0:4]
        mm = bank[4:6]
        fold_ps = bank[6]
        gather_ps = bank[7]

        def sem(name):
            return stack.enter_context(nc.semaphore(name))

        def sems(name, n):
            return [sem(f"{name}{i}") for i in range(n)]

        landed = sems("landed", SLOTS)
        used = sems("used", SLOTS)
        full = sems("bank_full", 8)
        read = sems("bank_read", 8)
        l_c, l_x, l_norm, l_aa, l_up, l_abias, l_glan, l_conv = (
            sem(f"load_{n}") for n in ("c", "x", "norm", "aa", "up", "abias", "glan", "conv"))
        l_bias4, l_bias = sem("load_ada_bias4"), sems("load_ada_bias", 2)
        l_xres, l_norm2, l_router, l_bgu, l_bdn, l_fin, stored = (
            sem(n) for n in ("load_xres", "load_norm2", "load_router", "load_bgu", "load_bdn", "load_fin", "stored"))
        pool_step = sem("pool_step")
        step, at_step = [0], {}
        c_sigd, c_silud, c_ready = sem("c_sigmoid"), sem("c_silu"), sem("c_cols")
        ada_used = sem("ada_bias_used")
        ada_part = sem("ada_partial")
        mod_ready = sem("mod_ready")
        sq_done, rs_sqrt, rs_done, hn_step, hn_ready = (
            sem(n) for n in ("squares", "roots", "rstd_ready", "hn_scaled", "hn_ready"))
        z_step, e_step, ln_step, la_ready = (sem(n) for n in ("z_step", "exp_step", "ln_step", "la_ready"))
        k_ready, bx, qd_ready = sem("k_end_ready"), sem("b_exp"), sem("qk_decayed")
        conv_step, yconv, st_step, sc_zero = (
            sem(n) for n in ("conv_step", "y_conv", "state_step", "scores_zeroed"))
        o_step, o_sum, o_root, r_sig, r_silu, y_ready = (
            sem(n) for n in ("o_step", "o_sum", "o_root", "r_sigmoid", "r_silu", "y_rows"))
        h1_ready, h_sq, h_root, h_step, hn2_ready = (
            sem(n) for n in ("h1_ready", "h_sq", "h_root", "h_step", "hn2_ready"))
        rt, rt_exp, rt_sel, rt_pos, rt_own, rt_T, tab_ready, it_ready = (
            sem(n) for n in ("route_step", "route_exp", "selected", "positions", "owners", "routeT_ready",
                             "table_ready", "items_ready"))
        part_a, part_r, part_b, part_c = sem("part_0"), sem("part_0_rest"), sem("part_1"), sem("part_2")
        hi_done, lo_done = sem("w_hi_done"), sem("w_lo_done")
        rows_out, folded = sem("gu_rows_out"), sem("folded")
        biased, gate_c, up_c, sig_done, gated_s, actf, acth, act_ready = (
            sem(n) for n in ("gu_biased", "gate_clamped", "up_clamped", "sigmoid", "gated", "act_full",
                                  "act_hi", "act_ready"))
        scattered, turned, put_ready, slot_w_ready = (
            sem(n) for n in ("scattered", "pick_turned", "put_ready", "slot_w_ready"))
        pick_ready, pickw_ready = sem("pick_ready"), sem("pick_w_ready")
        gathered, xs_hi_s, xs_ready = sem("gathered"), sem("xs_hi_ready"), sem("xs_ready")
        yhi_s, ylo_s = sems("y_hi_ready", 2), sems("y_lo_ready", 2)
        f_step, f_sq, f_root = sem("final_step"), sem("final_sq"), sem("final_root")

        def await_bank(eng, name):
            b, n = JOBS[name]
            if n:
                eng.wait_ge(read[b], n)
            return bank[b]

        def await_job(eng, name):
            b, n = JOBS[name]
            eng.wait_ge(full[b], n + 1)
            return bank[b]

        def after_job(eng, name):
            b, n = JOBS[name]
            eng.wait_ge(full[b], n + 1)

        def filled(ins, name):
            ins.then_inc(full[JOBS[name][0]], 1)

        def was_read(ins, name):
            ins.then_inc(read[JOBS[name][0]], 1)

        def after_read(eng, name):
            b, n = JOBS[name]
            eng.wait_ge(read[b], n + 1)

        def tok(g):
            return lambda k: hnT[:, g // 2, k, (g % 2) * P:(g % 2 + 1) * P]

        block = stack.enter_context(nc.Block())

        @block.sync
        def _(sp):
            source = {"ada": w_ada[0], "in": w_in[0], "out": w_out[0]}
            sp.dma_start(c_rows[0:KC, :], c[0].rearrange("(k p) -> k p", p=P)).then_inc(l_c, 16)
            sp.dma_start(c_rows[KC:2 * KC, :], c_ctx.rearrange("(k p) -> k p", p=P)).then_inc(l_c, 16)
            for t, (what, col) in enumerate(HEAD_TILES):
                j, n = head_slot(t), head_nth(t)
                if n:
                    after_job(sp, LAST_JOB[t - SLOTS])
                sp.dma_start(ring[:, j], source[what].rearrange("(k p) n -> p k n", p=P)[:, :, col:col + NT])\
                    .then_inc(landed[j], 16)
                if t in (2, 3):
                    half, src = t - 2, (x, ctx_tok)[t - 2]
                    sp.dma_start(x_mix[half * 64:half * 64 + 64], src[0].rearrange("(m p) n -> p m n", p=64))\
                        .then_inc(l_x, 16)
            for j in range(SLOTS):
                after_job(sp, LAST_JOB[NHEAD - SLOTS + j])
                w, col = (w_gu, NT * j) if j < GU else (w_dn, NT * (j - GU))
                sp.dma_start(ring[:, j], w[0, 0].rearrange("(k p) n -> p k n", p=P)[:, :, col:col + NT])\
                    .then_inc(landed[j], 16)
            sp.wait_ge(tab_ready, 1)
            n_items = sp.value_load(table[0:1, ICOLS:ICOLS + 1], min_val=1, max_val=ITEMS)
            with sp.Fori(0, GROUPS) as g:
                with sp.If(g * GROUP + 1 < n_items):
                    with sp.Fori(0, GROUP) as r:
                        i = sp.snap(g * GROUP + r + 1)
                        with sp.If(i < n_items):
                            e = sp.value_load(table[0:1, bass.ds(i, 1)], min_val=0, max_val=E - 1)
                            for j in range(SLOTS):
                                w = w_gu if j < GU else w_dn
                                col = NT * (j if j < GU else j - GU)
                                sp.wait_ge(used[j], i + 1)
                                sp.dma_start(ring[:, j], w[0][bass.ds(e, 1)].rearrange("e (k p) n -> p (e k) n", p=P)
                                             [:, :, col:col + NT]).then_inc(landed[j], 16)
            for j in range(SLOTS):
                sp.wait_ge(used[j], n_items + 1)
            sp.dma_start(fin_n[:, :], final_norm_w.partition_broadcast(P)).then_inc(l_fin, 16)
            for t in range(2):
                sp.wait_ge(f_step, 10 + 2 * t)
                sp.dma_start(out[0, t * P:(t + 1) * P, :], fin_y[:, t, :]).then_inc(stored, 16)
            sp.wait_ge(stored, 32)

        @block.gpsimd
        def _(pool):
            def made(ins, name=None):
                step[0] += 1
                ins.then_inc(pool_step, 1)
                pool.wait_ge(pool_step, step[0])
                if name:
                    at_step[name] = step[0]

            def select(view, op, base_, pattern, mult, fill):
                return pool.affine_select(out=view, in_=view, compare_op=op, fill=fill, base=base_,
                                          pattern=pattern, channel_multiplier=mult)

            made(pool.memset(ident[:, :], 0.0))
            made(pool.memset(ones[:, :], 1.0))
            made(pool.memset(eps_col[:, :], EPS))
            made(pool.memset(one_col[:, :], 1.0))
            made(select(ident[:, :], ALU.not_equal, 0, [[-1, P]], 1, 1.0), "ident")
            pool.dma_start(ada_bias4[:, :, :].rearrange("p t n -> p (t n)"), b_ada[0, 0:4 * NT].partition_broadcast(P))\
                .then_inc(l_bias4, 16)
            pool.dma_start(norm_bc[:, :], norm1_w[0].partition_broadcast(P)).then_inc(l_norm, 16)
            pool.dma_start(w_aa[:, :, :], w_in[0].rearrange("(k p) n -> p k n", p=P)[:, :, AF0:AF0 + 2 * RANK])\
                .then_inc(l_aa, 16)
            for m in (up_to, beyond):
                made(pool.memset(m[:, :, :], 1.0 / GATE_NORM))
            made(pool.memset(in_chunk[:, :], 0.0))
            made(select(up_to[:, 0, :], ALU.is_ge, 0, [[1, P]], -1, 0.0))
            made(select(up_to[:, 1, :], ALU.is_ge, 0, [[-1, P]], 1, 0.0))
            made(select(beyond[:, 0, :], ALU.is_gt, 0, [[-1, P]], 1, 0.0))
            made(select(beyond[:, 1, :], ALU.is_gt, 0, [[1, P]], -1, 0.0))
            for m in (up_to, beyond):
                made(pool.memset(m[0:CH, :, CH:P], 0.0))
                made(pool.memset(m[CH:P, :, 0:CH], 0.0))
            made(pool.memset(in_chunk[0:CH, 0:1], 1.0 / GATE_NORM))
            made(pool.memset(in_chunk[CH:P, 1:2], 1.0 / GATE_NORM))
            made(pool.iota(slot_no[:, :, :], pattern=[[0, 2], [1, TOK]], base=1, channel_multiplier=0,
                      allow_small_or_imprecise_dtypes=True))
            made(pool.memset(fold[:, :], 0.0))
            for half in range(2):
                rows = fold[half * TOK:(half + 1) * TOK, :]
                made(select(rows, ALU.not_equal, 0, [[-1, TOK]], 1, 1.0), "scan")
            pool.wait_ge(l_x, 32)
            for t in (4, 5):
                pool.dma_start(ada_bias[:, t % 2, :], b_ada[0, t * NT:(t + 1) * NT].partition_broadcast(P))\
                    .then_inc(l_bias[t % 2], 16)
            made(pool.memset(up_blk[:, :], 0.0))
            pool.dma_start(up_blk[0:RANK, 0:QK], a_up_f[0]).then_inc(l_up, 16)
            pool.dma_start(up_blk[RANK:2 * RANK, QK:2 * QK], a_up_b[0]).then_inc(l_up, 16)
            pool.dma_start(a_bias[:, 0:QK], a_bias_f[0].partition_broadcast(P)).then_inc(l_abias, 16)
            pool.dma_start(a_bias[:, QK:2 * QK], a_bias_b[0].partition_broadcast(P)).then_inc(l_abias, 16)
            pool.dma_start(glan_bc[:, :], gla_norm_w[0].partition_broadcast(P)).then_inc(l_glan, 16)
            with nc.allow_non_contiguous_dma(reason="conv taps, by channel"):
                for tap in range(3):
                    pool.dma_start(conv_k[:, tap, :], conv_w[0, tap].rearrange("(f p) -> p f", p=P))\
                        .then_inc(l_conv, 16)
            pool.wait_ge(mod_ready, 1)
            pool.dma_start(norm_bc[:, :], norm2_w[0].partition_broadcast(P)).then_inc(l_norm2, 16)
            pool.wait_ge(z_step, 4)
            made(pool.memset(keep[:, :, :, :], 1.0))
            for half in range(2):
                rows = keep[half * CH:(half + 1) * CH]
                made(select(rows[:, :, 0, :], ALU.is_ge, 0, [[0, HEADS], [1, CH]], -1, 0.0))
                made(select(rows[:, :, 1, :], ALU.is_ge, 0, [[0, HEADS], [-1, CH]], 1, 0.0), "keep")
            for t in range(6, 12):
                pool.wait_ge(ada_used, t - 1)
                pool.dma_start(ada_bias[:, t % 2, :], b_ada[0, t * NT:(t + 1) * NT].partition_broadcast(P))\
                    .then_inc(l_bias[t % 2], 16)
                if t == 10:
                    pool.wait_ge(y_ready, 2)
                    pool.dma_start(h1[:, :, :], x[0].rearrange("(t p) n -> p t n", p=P)).then_inc(l_xres, 16)
                    after_job(pool, "yT1")
                    pool.dma_start(bgu_rows[:, :], b_gu[0]).then_inc(l_bgu, 16)
            pool.dma_start(r_w[:, :, :], router_w[0].rearrange("(k p) e -> p k e", p=P)).then_inc(l_router, 16)
            pool.dma_start(r_b[:, :], router_b[0].partition_broadcast(P)).then_inc(l_router, 16)
            exact = dict(allow_small_or_imprecise_dtypes=True)
            made(pool.iota(e_no[:, :], pattern=[[1, E]], base=0, channel_multiplier=0, **exact))
            made(pool.iota(i_no[:, :], pattern=[[1, ICOLS]], base=0, channel_multiplier=0, **exact))
            made(pool.iota(i_no64[:, :], pattern=[[TOK, ICOLS]], base=0, channel_multiplier=0, **exact))
            made(pool.iota(limits[:, :], pattern=[[TOK, 3]], base=TOK, channel_multiplier=0, **exact))
            made(pool.iota(e_col[:, :], pattern=[[0, 1]], base=0, channel_multiplier=1, **exact))
            made(pool.memset(below[:, :], 1.0))
            made(pool.memset(tri[:, :], 1.0))
            made(select(below[:, :], ALU.is_gt, 0, [[1, E]], -1, 0.0))
            made(select(tri[:, :], ALU.is_ge, 0, [[1, P]], -1, 0.0), "tables")
            after_job(pool, "h2T11")
            pool.wait_ge(part_r, 2)
            pool.dma_start(bdn_rows[:, :], b_dn[0]).then_inc(l_bdn, 16)

        @block.scalar
        def _(act):
            def copy(o, i):
                return act.activation(o, i, ACT.Copy)

            act.wait_ge(l_c, 32)
            act.activation(c_sig[:, :], c_rows[:, :], ACT.Sigmoid).then_inc(c_sigd, 1)
            act.wait_ge(l_x, 32)
            for m in range(4):
                act.activation(hnT[:, 0, 4 * (m % 2):4 * (m % 2) + 4, :], x_mix[:, m, :].rearrange("p (a b) -> p a b", a=4),
                               ACT.Square, accum_out=sums[:, m:m + 1]).then_inc(sq_done, 1)
                act.wait_ge(sq_done, m + 1)
            act.wait_ge(pool_step, at_step["ident"])
            act.activation(rstd[:, 0:4], sums[:, 0:4], ACT.Sqrt, bias=eps_col[:, 0:1], scale=1.0 / D)\
                .then_inc(rs_sqrt, 1)
            for m in range(4):
                for half in range(2):
                    ps = await_job(act, f"hnT{m}{half}")
                    src = ps[:, :].rearrange("p (k s t) -> p s k t", k=4, s=2)
                    for s in range(2):
                        ins = copy(hnT[:, s, 4 * half:4 * half + 4, m * 64:(m + 1) * 64], src[:, s])
                        if s:
                            was_read(ins, f"hnT{m}{half}")
            ps = await_job(act, "aa")
            was_read(copy(aT[:, :], ps[0:2 * RANK, :]), "aa")
            for g in range(4):
                ps = await_job(act, f"qk{g}")
                if g < 2:
                    was_read(copy(qk_rows[:, g, :], ps[:, :]), f"qk{g}")
                else:
                    was_read(copy(k_ctx[:, g - 2, :], ps[:, 0:QK]), f"qk{g}")
            for g in range(4):
                act.wait_ge(z_step, 4 + g + 1)
                act.activation(la[:, g, :], la[:, g, :], ACT.Exp).then_inc(e_step, 1)
            for g in range(4):
                act.wait_ge(e_step, g + 1)
                act.activation(la[:, g, :], la[:, g, :], ACT.Ln, bias=one_col[:, 0:1]).then_inc(ln_step, 1)
            for g in range(4):
                ps = await_job(act, f"v{g}")
                was_read(copy(v_rows[:, g, :], ps[:, :]), f"v{g}")
            for g in range(4):
                ps = await_job(act, f"kp{g}")
                was_read(act.activation(k_end[:, g], ps[:, :].rearrange("p (d n) -> p d n", d=2), ACT.Exp), f"kp{g}")
            ps = await_job(act, "dec")
            was_read(act.activation(decay[:, :, :].rearrange("p d (g h) -> p d g h", g=4),
                                    ps[:, 0:32].rearrange("p (g dp h) -> p dp g h", g=4, dp=4),
                                    ACT.Exp), "dec")
            for t in range(2):
                ps = await_job(act, f"bT{t}")
                src = ps[:, :].rearrange("p (d t) -> p d t", d=4)
                if t == 0:
                    act.wait_ge(full[JOBS["bT1"][0]], JOBS["bT1"][1] + 1)
                act.activation(q_dec[:, :, t * P:(t + 1) * P], src, ACT.Exp).then_inc(bx, 1)
                was_read(act.activation(k_inv[:, :, t * P:(t + 1) * P], src, ACT.Exp, scale=-1.0), f"bT{t}")
            for t in range(2):
                ps = await_job(act, f"r{t}")
                was_read(copy(r_rows[:, t, :], ps[:, :]), f"r{t}")
            for half in range(2):
                ps = await_job(act, f"c{half}")
                was_read(copy(conv_u[:, 2 * half:2 * half + 2, :], ps[:, :].rearrange("p (f t) -> p f t", f=2)),
                         f"c{half}")
            after_job(act, "qkT1")
            act.wait_ge(k_ready, 4)
            for t in range(2):
                after_read(act, f"r{t}")
                act.activation(qk_rows[:, t, :], r_rows[:, t, :], ACT.Sigmoid).then_inc(r_sig, 1)
            for t in range(2):
                ps = await_job(act, f"oi{t}")
                if t == 0:
                    act.wait_ge(yconv, 2)
                was_read(copy(o_rows[:, t, :], ps[:, :]), f"oi{t}")
            act.wait_ge(o_sum, 2)
            act.activation(rstd[:, 4:12], sums[:, 4:12], ACT.Sqrt, bias=eps_col[:, 0:1], scale=1.0 / DV)\
                .then_inc(o_root, 1)
            for t in range(2):
                ps = await_job(act, f"yT{t}")
                was_read(copy(yT[:, 0:4, t * P:(t + 1) * P], ps[:, :].rearrange("p (f t) -> p f t", f=4)), f"yT{t}")
            act.activation(rstd[:, 12:13], eps_col[:, 0:1], ACT.Sqrt).then_inc(h_sq, 1)
            act.wait_ge(h_sq, 1)
            for t in range(2):
                act.wait_ge(h1_ready, 3 + t)
                act.activation(hn2[:, t, :], h1[:, t, :], ACT.Square, accum_out=sums[:, 12 + t:13 + t])\
                    .then_inc(h_sq, 1)
                act.wait_ge(h_sq, 2 + t)
                act.activation(rstd[:, 12 + t:13 + t], sums[:, 12 + t:13 + t], ACT.Sqrt, bias=eps_col[:, 0:1],
                               scale=1.0 / D).then_inc(h_root, 1)
            for t in range(2):
                act.wait_ge(hn2_ready, t + 1)
                copy(hn2_parts[:, t, 0, :], hn2[:, t, :]).then_inc(part_a, 1)
                for half in range(2):
                    ps = await_job(act, f"h2T{t}{half}")
                    was_read(copy(h2T[:, 4 * half:4 * half + 4, t * P:(t + 1) * P],
                                  ps[:, :].rearrange("p (k t) -> p k t", k=4)), f"h2T{t}{half}")
            act.wait_ge(rt, 3)
            act.activation(soft[:, :, :], soft[:, :, :], ACT.Exp).then_inc(rt_exp, 1)
            for t in range(2):
                act.wait_ge(part_r, t + 1)
                copy(hn2_parts[:, t, 1, :], resid[:, t, :]).then_inc(part_b, 1)
            def xs_first():
                copy(xs[:, :, 0:TOK], gather_ps[:, :].rearrange("p (k m) -> p k m", k=KC)).then_inc(xs_hi_s, 1)

            def y_first(h):
                act.activation(y_hi[:, h * NT:(h + 1) * NT], mm[h][:, :], ACT.Copy, scale=slot_w[:, 0:1])\
                    .then_inc(yhi_s[h], 1)

            act.activation(sums[:, 0:1], eps_col[:, 0:1], ACT.Sigmoid)
            ps = await_job(act, "bias0")
            was_read(copy(bias_items[:, 0:8, :], ps[:, 0:8 * ICOLS].rearrange("p (f i) -> p f i", f=8)), "bias0")
            act.wait_ge(gathered, 1)
            xs_first()
            act.wait_ge(tab_ready, 1)
            n_items = act.value_load(table[0:1, ICOLS:ICOLS + 1], min_val=1, max_val=ITEMS)
            with act.Fori(0, GROUPS) as g:
                with act.If(g * GROUP < n_items):
                    with act.Fori(0, GROUP) as r:
                        i = act.snap(g * GROUP + r)
                        with act.If(i < n_items):
                            i4 = act.snap(i * GU)

                            def halve(j, pieces=range(2)):
                                act.wait_ge(landed[j], 16 * (i + HEAD_USES[j] + 1))
                                b = (j - HI_BUFS) % SLOTS
                                act.wait_ge(used[b], i + (2 if j >= HI_BUFS else 1))
                                for p in pieces:
                                    k = WHOLE + p * PIECE
                                    copy(w_hi[:, j % HI_BUFS, p], ring[:, j, k:k + PIECE, :]).then_inc(hi_done, 1)

                            def rows(j):
                                act.wait_ge(used[j], i + 2)
                                copy(gu_rows[:, j * NT:(j + 1) * NT], mm[j % 2][:, :]).then_inc(rows_out, 1)

                            def sigmoid(j):
                                act.wait_ge(gate_c, i4 + j + 1)
                                act.activation(sig[:, j % 2], gu_c[:, j % 2, 0:2, :], ACT.Sigmoid, scale=ALPHA)\
                                    .then_inc(sig_done, 1)

                            halve(0, (0,))
                            act.wait_ge(used[4], i + 1)
                            act.wait_ge(slot_w_ready, i + 1)
                            y_first(0)
                            halve(0, (1,))
                            halve(1)
                            act.wait_ge(used[5], i + 1)
                            y_first(1)
                            halve(2)
                            rows(0)
                            halve(3)
                            rows(1)
                            sigmoid(0)
                            halve(4)
                            rows(2)
                            sigmoid(1)
                            act.wait_ge(turned, i + 1)
                            copy(put[:, :], gather_ps[:, 0:SEQ]).then_inc(put_ready, 1)
                            copy(slot_w[:, :], gather_ps[:, SEQ:SEQ + 1]).then_inc(slot_w_ready, 1)
                            sigmoid(2)
                            halve(5)
                            rows(3)
                            sigmoid(3)
                            act.wait_ge(gathered, i + 2)
                            xs_first()
            for j in range(SLOTS):
                act.wait_ge(used[j], n_items + 1)
            act.wait_ge(slot_w_ready, n_items + 1)
            y_first(0)
            y_first(1)
            act.activation(rstd_f[:, 0:2], eps_col[:, 0:1].broadcast_to([P, 2]), ACT.Sqrt).then_inc(f_sq, 1)
            act.wait_ge(f_sq, 1)
            for t in range(2):
                act.wait_ge(f_step, 4 * (t + 1))
                act.activation(fin_sq[:, t, :], fin_y[:, t, :], ACT.Square, accum_out=sums_f[:, t:t + 1])\
                    .then_inc(f_sq, 1)
                act.wait_ge(f_sq, 2 + t)
                act.activation(rstd_f[:, t:t + 1], sums_f[:, t:t + 1], ACT.Sqrt, bias=eps_col[:, 0:1], scale=1.0 / D)\
                    .then_inc(f_root, 1)

        @block.vector
        def _(dve):
            dve.wait_ge(c_sigd, 1)
            dve.tensor_tensor(c_rows[:, :], c_rows[:, :], c_sig[:, :], ALU.mult).then_inc(c_silud, 1)
            ps = await_job(dve, "cT")
            dve.tensor_copy(c_mix[:, :, :, :], ps[:, 0:2 * KC].rearrange("p (s k) -> p k s", s=2)
                            .unsqueeze(3).broadcast_to([P, KC, 2, 64])).then_inc(c_ready, 1)
            was_read(dve.tensor_copy(c_all[:, :, :], ps[:, 0:KC].unsqueeze(2).broadcast_to([P, KC, P])), "cT")

            def landed_bias(t):
                if t < 4:
                    dve.wait_ge(l_bias4, 16)
                    return ada_bias4[:, t, :]
                dve.wait_ge(l_bias[t % 2], 16 * (t // 2 - 1))
                return ada_bias[:, t % 2, :]

            def ada_add(t, dst):
                ps = await_job(dve, f"ada{t}")
                was_read(dve.tensor_tensor(dst, ps[:, :], landed_bias(t), ALU.add), f"ada{t}")
                after_read(dve, f"ada{t}")
                dve.engine_nop().then_inc(ada_used, 1)

            def ada_scale(t, dst, cols):
                ps = await_job(dve, f"ada{t}")
                was_read(dve.scalar_tensor_tensor(out=dst, in0=ps[:, :], scalar=1.0, in1=landed_bias(t),
                                                  op0=ALU.add, op1=ALU.add), f"ada{t}")
                after_read(dve, f"ada{t}")
                ins = dve.tensor_tensor(dst, dst, norm_bc[:, cols], ALU.mult)
                ins.then_inc(ada_used, 1)

            def ada_partial(a):
                t = HEAD_TILES.index(ADA[a])
                dve.wait_ge(landed[head_slot(t)], 16 * (head_nth(t) + 1))
                tile = ring[:, head_slot(t)]
                dve.tensor_scalar(tile[:, 0, :], tile[:, 0, :], c_all[:, 0, 0:1], None, ALU.mult)\
                    .then_inc(ada_part, 1)
                for k in range(1, KC):
                    dve.wait_ge(ada_part, KC * (a - 5) + k)
                    dve.scalar_tensor_tensor(out=tile[:, 0, :], in0=tile[:, k, :], scalar=c_all[:, k, 0:1],
                                             in1=tile[:, 0, :], op0=ALU.mult, op1=ALU.add).then_inc(ada_part, 1)

            for t in range(2):
                ada_add(t, mod[:, 1, t * NT:(t + 1) * NT])
            dve.wait_ge(l_norm, 16)
            for t in range(2):
                ada_scale(2 + t, mod[:, 0, t * NT:(t + 1) * NT], slice(t * NT, (t + 1) * NT))
            dve.wait_ge(rs_sqrt, 1)
            dve.reciprocal(rstd[:, 0:4], rstd[:, 0:4]).then_inc(rs_done, 1)
            dve.wait_ge(rs_done, 1)
            dve.wait_ge(ada_used, 4)
            dve.engine_nop().then_inc(mod_ready, 1)
            for m in range(4):
                dve.scalar_tensor_tensor(out=x_mix[:, m, :], in0=x_mix[:, m, :], scalar=rstd[:, m:m + 1],
                                         in1=mod[:, 0, :], op0=ALU.mult, op1=ALU.mult).then_inc(hn_step, 1)
                dve.wait_ge(hn_step, m + 1)
                dve.tensor_tensor(x_mix[:, m, :], x_mix[:, m, :], mod[:, 1, :], ALU.add).then_inc(hn_ready, 1)

            ada_add(4, g1_bc[:, 0:NT])
            ada_partial(5)
            ada_partial(6)

            def zrow(g):
                return k_end[:, g].rearrange("p d n -> p (d n)")

            dve.wait_ge(l_abias, 32)
            for g in range(4):
                ps = await_job(dve, f"z{g}")
                was_read(dve.tensor_tensor(zrow(g), ps[:, :], a_bias[:, :], ALU.add), f"z{g}")
                after_read(dve, f"z{g}")
                dve.engine_nop().then_inc(z_step, 1)
            for g in range(4):
                dve.scalar_tensor_tensor(out=la[:, g, :], in0=zrow(g), scalar=-1.0, in1=zrow(g),
                                         op0=ALU.mult, op1=ALU.min).then_inc(z_step, 1)
            for g in range(4):
                dve.wait_ge(ln_step, g + 1)
                dve.scalar_tensor_tensor(out=la[:, g, :], in0=zrow(g), scalar=0.0, in1=la[:, g, :],
                                         op0=ALU.min, op1=ALU.subtract).then_inc(la_ready, 1)
            ada_add(5, g1_bc[:, NT:2 * NT])
            ada_partial(7)
            ada_add(6, mod[:, 1, 0:NT])
            ada_partial(8)
            for g in range(4):
                after_read(dve, f"kp{g}")
                after_read(dve, f"qk{g}")
                k_row = qk_rows[:, g, QK:2 * QK] if g < 2 else k_ctx[:, g - 2, :]
                dve.tensor_tensor(k_end[:, g], k_end[:, g], k_row.unsqueeze(1).broadcast_to([P, 2, QK]), ALU.mult)\
                    .then_inc(k_ready, 1)
            ada_add(7, mod[:, 1, NT:2 * NT])
            ada_partial(9)
            dve.wait_ge(l_norm2, 16)
            ada_scale(8, mod[:, 0, 0:NT], slice(0, NT))
            for t in range(2):
                ps = await_job(dve, f"qkT{t}")
                after_read(dve, f"bT{t}")
                dve.wait_ge(bx, t + 1)
                for d in range(2):
                    dst = q_dec[:, 2 * d:2 * d + 2, t * P:(t + 1) * P]
                    dve.scalar_tensor_tensor(out=dst, in0=ps[:, 0:256].rearrange("p (a t) -> p a t", a=2),
                                             scalar=DK ** -0.5, in1=dst, op0=ALU.mult, op1=ALU.mult)\
                        .then_inc(qd_ready, 1)
                    dst = k_inv[:, 2 * d:2 * d + 2, t * P:(t + 1) * P]
                    ins = dve.tensor_tensor(dst, ps[:, 256:512].rearrange("p (a t) -> p a t", a=2), dst, ALU.mult)
                    if d == 0:
                        ins.then_inc(qd_ready, 1)
                    else:
                        was_read(ins, f"qkT{t}")
            after_read(dve, "dec")

            def state_step(s):
                for dp in range(4):
                    fwd = dp < 2
                    name = f"kvf{s}" if fwd else f"kvb{s}"
                    ps = await_job(dve, name)
                    kv = ps[:, dp % 2 * DV:(dp % 2 + 1) * DV]
                    if s < 4:
                        ch = s if fwd else 3 - s
                        dst = src = states[:, dp, 0 if fwd else 3, :]
                        dec = decay[:, dp, 4 + ch:5 + ch]
                    else:
                        ch = s - 4 if fwd else 7 - s
                        src = states[:, dp, ch, :]
                        dst = states[:, dp, ch + 1 if fwd else ch - 1, :]
                        dec = decay[:, dp, ch:ch + 1]
                    if s == 0:
                        ins = dve.tensor_copy(dst, kv)
                    else:
                        dve.wait_ge(st_step, 2 * s)
                        after_read(dve, f"kvf{s - 1}")
                        after_read(dve, f"kvb{s - 1}")
                        ins = dve.scalar_tensor_tensor(out=dst, in0=src, scalar=dec, in1=kv,
                                                       op0=ALU.mult, op1=ALU.add)
                    if dp % 2 == 0:
                        ins.then_inc(st_step, 1)
                    else:
                        was_read(ins, name)

            state_step(0)
            state_step(1)
            for t in range(2):
                dve.wait_ge(r_sig, t + 1)
                dve.tensor_tensor(r_rows[:, t, :], r_rows[:, t, :], qk_rows[:, t, :], ALU.mult).then_inc(r_silu, 1)
            dve.wait_ge(ada_used, 4)
            dve.memset(scores[:, :, :, :, :], 0.0).then_inc(sc_zero, 1)
            dve.wait_ge(l_conv, 48)
            for half in range(2):
                ps = await_job(dve, f"x{half}")
                after_read(dve, f"c{half}")
                u = conv_u[:, 2 * half:2 * half + 2, :]
                was_read(dve.tensor_tensor(u, ps[:, :].rearrange("p (f t) -> p f t", f=2), u, ALU.mult), f"x{half}")
                state_step(2 + half)
            for half in range(2):
                after_read(dve, f"x{half}")
            n_conv = 0
            for f in range(4):
                dve.tensor_scalar(conv_y[:, f, :], conv_u[:, f, :], conv_k[:, 1, f:f + 1], None, ALU.mult)\
                    .then_inc(conv_step, 1)
            for tap, (lo, hi) in ((0, (1, 0)), (2, (0, 1))):
                n_conv += 4
                for f in range(4):
                    dve.wait_ge(conv_step, n_conv - 3 + f)
                    dst = conv_y[:, f, :].rearrange("p (r w) -> p r w", w=GRID_W)[:, :, lo:GRID_W - hi]
                    src = conv_u[:, f, :].rearrange("p (r w) -> p r w", w=GRID_W)[:, :, hi:GRID_W - lo]
                    dve.scalar_tensor_tensor(out=dst, in0=src, scalar=conv_k[:, tap, f:f + 1], in1=dst,
                                             op0=ALU.mult, op1=ALU.add).then_inc(conv_step, 1)
            dve.wait_ge(conv_step, 12)
            for half in range(2):
                ps = await_job(dve, f"b{half}")
                was_read(dve.tensor_tensor(yT[:, 4 + 2 * half:6 + 2 * half, :],
                                           ps[:, :].rearrange("p (f t) -> p f t", f=2),
                                           conv_y[:, 2 * half:2 * half + 2, :], ALU.mult), f"b{half}")
                after_read(dve, f"b{half}")
                dve.engine_nop().then_inc(yconv, 1)
                state_step(4 + half)
            state_step(6)
            dve.wait_ge(sc_zero, 1)
            dve.wait_ge(pool_step, at_step["keep"])
            for t in range(2):
                for odd, name in enumerate((f"sce{t}", f"sco{t}")):
                    ps = await_job(dve, name)
                    was_read(dve.copy_predicated(
                        scores[:, t, odd:HEADS:2].rearrange("p h d t -> p h (d t)"),
                        keep[:, odd:HEADS:2].rearrange("p h d t -> p h (d t)").bitcast(I32),
                        ps[:, 0:2 * P].rearrange("p (h n) -> p h n", h=2)), name)
            dve.wait_ge(l_glan, 16)
            for t in range(2):
                after_read(dve, f"oi{t}")
                for odd, name in enumerate((f"oe{t}", f"oo{t}")):
                    ps = await_job(dve, name)
                    dst = o_rows[:, t, :].rearrange("p (h v) -> p h v", h=HEADS)[:, odd:HEADS:2, :]
                    was_read(dve.tensor_tensor(dst, ps[:, 0:2 * DV].rearrange("p (h v) -> p h v", h=2), dst, ALU.add),
                             name)
                after_read(dve, f"oe{t}")
                after_read(dve, f"oo{t}")
                dve.tensor_tensor(o_sq[:, t, :], o_rows[:, t, :], o_rows[:, t, :], ALU.mult).then_inc(o_step, 1)
            for t in range(2):
                dve.wait_ge(o_step, t + 1)
                dve.tensor_reduce(sums[:, 4 + 4 * t:8 + 4 * t], o_sq[:, t, :].rearrange("p (h v) -> p h v", h=HEADS),
                                  AX.X, ALU.add).then_inc(o_sum, 1)
            dve.wait_ge(o_root, 1)
            dve.reciprocal(rstd[:, 4:12], rstd[:, 4:12]).then_inc(o_step, 1)
            dve.wait_ge(o_step, 3)
            for t in range(2):
                view = o_rows[:, t, :].rearrange("p (h v) -> p h v", h=HEADS)
                dve.tensor_tensor(view, view, rstd[:, 4 + 4 * t:8 + 4 * t].unsqueeze(2).broadcast_to([P, HEADS, DV]),
                                  ALU.mult).then_inc(o_step, 1)
                dve.wait_ge(o_step, 4 + 2 * t)
                dve.tensor_tensor(view, view, glan_bc[:, :].unsqueeze(1).broadcast_to([P, HEADS, DV]), ALU.mult)\
                    .then_inc(o_step, 1)
                dve.wait_ge(o_step, 5 + 2 * t)
                dve.wait_ge(r_silu, t + 1)
                dve.tensor_tensor(o_rows[:, t, :], o_rows[:, t, :], r_rows[:, t, :], ALU.mult).then_inc(y_ready, 1)
            ada_scale(9, mod[:, 0, NT:2 * NT], slice(NT, 2 * NT))
            dve.wait_ge(l_xres, 16)
            for half in range(2):
                cols = slice(half * NT, (half + 1) * NT)
                for t in range(2):
                    n = 2 * half + t
                    ps = await_job(dve, f"wo{half}{t}")
                    if n:
                        dve.wait_ge(h1_ready, n)
                    was_read(dve.tensor_tensor(scaled[:, :], ps[:, :], g1_bc[:, cols], ALU.mult), f"wo{half}{t}")
                    after_read(dve, f"wo{half}{t}")
                    dve.tensor_tensor(h1[:, t, cols], h1[:, t, cols], scaled[:, :], ALU.add)\
                        .then_inc(h1_ready, 1)
            for t in range(2):
                dve.wait_ge(h_root, t + 1)
                dve.reciprocal(rstd[:, 12 + t:13 + t], rstd[:, 12 + t:13 + t]).then_inc(h_step, 1)
                dve.wait_ge(h_step, 2 * t + 1)
                dve.scalar_tensor_tensor(out=hn2[:, t, :], in0=h1[:, t, :], scalar=rstd[:, 12 + t:13 + t],
                                         in1=mod[:, 0, :], op0=ALU.mult, op1=ALU.mult).then_inc(h_step, 1)
                dve.wait_ge(h_step, 2 * t + 2)
                dve.tensor_tensor(hn2[:, t, :], hn2[:, t, :], mod[:, 1, :], ALU.add).then_inc(hn2_ready, 1)
            for t in range(2):
                dve.wait_ge(part_a, t + 1)
                dve.tensor_tensor(resid[:, t, :], hn2[:, t, :], hn2_parts[:, t, 0, :], ALU.subtract)\
                    .then_inc(part_r, 1)
            dve.tensor_copy(ident_bf[:, :], ident[:, :]).then_inc(part_r, 1)
            ada_add(10, g2_bc[:, 0:NT])
            ada_add(11, g2_bc[:, NT:2 * NT])
            dve.wait_ge(l_router, 32)
            ps = await_job(dve, "logits")
            was_read(dve.tensor_tensor(logit[:, :, :], ps[:, 0:2 * E].rearrange("p (t e) -> p t e", t=2),
                                       r_b[:, :].unsqueeze(1).broadcast_to([P, 2, E]), ALU.add), "logits")
            after_read(dve, "logits")
            for t in range(2):
                dve.max(top[:, t, :], logit[:, t, :]).then_inc(rt, 1)
            dve.wait_ge(rt, 2)
            dve.tensor_tensor(soft[:, :, :], top[:, :, 0:TOPK], top[:, :, 0:1].broadcast_to([P, 2, TOPK]),
                              ALU.subtract).then_inc(rt, 1)
            for t in range(2):
                dve.max_index(top_i[:, t, :], top[:, t, :], logit[:, t, :]).then_inc(rt, 1)
            dve.wait_ge(rt, 5)
            dve.tensor_copy(top_f[:, :, :], top_i[:, :, 0:TOPK]).then_inc(rt, 1)
            dve.wait_ge(rt, 6)
            dve.wait_ge(pool_step, at_step["tables"])
            dve.tensor_tensor(hot[:, :, :, :].rearrange("p t j e -> p (t j) e"),
                              e_no[:, :].unsqueeze(1).broadcast_to([P, 2 * TOPK, E]),
                              top_f[:, :, :].rearrange("p t j -> p (t j)").unsqueeze(2).broadcast_to([P, 2 * TOPK, E]),
                              ALU.is_equal).then_inc(rt, 1)
            dve.wait_ge(rt, 7)
            dve.tensor_reduce(sel[:, :, :], hot[:, :, :, :].rearrange("p t j e -> p t e j"), AX.X, ALU.add)\
                .then_inc(rt_sel, 1)
            dve.wait_ge(rt_exp, 1)
            dve.tensor_reduce(soft_s[:, :], soft[:, :, :], AX.X, ALU.add).then_inc(rt, 1)
            dve.wait_ge(rt, 8)
            dve.reciprocal(soft_r[:, :], soft_s[:, :]).then_inc(rt, 1)
            dve.wait_ge(rt, 9)
            dve.tensor_tensor(w_top[:, :, :], soft[:, :, :], soft_r[:, :].unsqueeze(2).broadcast_to([P, 2, TOPK]),
                              ALU.mult).then_inc(rt, 1)
            dve.wait_ge(rt, 10)
            dve.tensor_tensor(hot_w[:, :, :, :].rearrange("p t j e -> p (t j) e"),
                              hot[:, :, :, :].rearrange("p t j e -> p (t j) e"),
                              w_top[:, :, :].rearrange("p t j -> p (t j)").unsqueeze(2).broadcast_to([P, 2 * TOPK, E]),
                              ALU.mult).then_inc(rt, 1)
            dve.wait_ge(rt, 11)
            dve.tensor_reduce(w_full[:, :, :], hot_w[:, :, :, :].rearrange("p t j e -> p t e j"), AX.X, ALU.add)\
                .then_inc(rt_pos, 1)
            ps = await_job(dve, "rank")
            dve.wait_ge(rt_sel, 1)
            dve.tensor_tensor(pos[:, :, :], ps[:, 0:2 * E].rearrange("p (t e) -> p t e", t=2), sel[:, :, :], ALU.mult)\
                .then_inc(rt_pos, 1)
            dve.tensor_scalar(more[:, :], limits[:, :], ps[0:E, 64:65], None, ALU.is_lt).then_inc(rt, 1)
            dve.wait_ge(rt, 12)
            dve.tensor_reduce(tiles_e[:, :], more[:, :], AX.X, ALU.add).then_inc(rt, 1)
            dve.wait_ge(rt, 13)
            was_read(dve.tensor_scalar(tiles_e[:, :], tiles_e[:, :], 1.0, None, ALU.add), "rank")
            ps = await_job(dve, "start")
            after_read(dve, "rank")
            dve.tensor_copy(begin_e[:, 0:1], ps[0:E, 0:1]).then_inc(rt_own, 1)
            dve.tensor_tensor(begin_e[:, 1:2], ps[0:E, 0:1], tiles_e[:, :], ALU.add).then_inc(rt_own, 1)
            dve.tensor_scalar(begin_e[:, 2:3], ps[0:E, 0:1], float(TOK), None, ALU.mult).then_inc(rt_own, 1)
            dve.tensor_copy(table[0:1, ICOLS:ICOLS + 1], ps[0:1, 1:2]).then_inc(rt_own, 1)
            dve.wait_ge(rt_own, 4)
            dve.tensor_scalar(own[:, :], i_no[0:E, :], begin_e[:, 0:1], None, ALU.is_ge).then_inc(rt_own, 1)
            dve.wait_ge(rt_own, 5)
            dve.scalar_tensor_tensor(out=own[:, :], in0=i_no[0:E, :], scalar=begin_e[:, 1:2], in1=own[:, :],
                                     op0=ALU.is_lt, op1=ALU.mult).then_inc(rt_own, 1)
            ps = await_job(dve, "turn")
            dve.tensor_scalar(routeT[:, 0, :], ps[0:E, 0:SEQ], begin_e[:, 2:3], None, ALU.add).then_inc(rt_T, 1)
            was_read(dve.tensor_copy(routeT[:, 1, :], ps[0:E, SEQ:2 * SEQ]), "turn")
            for t in range(2):
                dve.wait_ge(part_b, t + 1)
                dve.tensor_tensor(hn2_parts[:, t, 2, :], resid[:, t, :], hn2_parts[:, t, 1, :], ALU.subtract)\
                    .then_inc(part_c, 1)
            ps = await_job(dve, "items")
            dve.tensor_copy(table[0:1, 0:ICOLS], ps[0:1, 4 * ICOLS:5 * ICOLS]).then_inc(tab_ready, 1)
            dve.tensor_tensor(item_pos[:, :, :], ps[:, 0:2 * ICOLS].rearrange("p (t i) -> p t i", t=2),
                              i_no64[:, :].unsqueeze(1).broadcast_to([P, 2, ICOLS]), ALU.subtract)\
                .then_inc(it_ready, 1)
            was_read(dve.tensor_copy(item_w[:, :, :], ps[:, 2 * ICOLS:4 * ICOLS].rearrange("p (t i) -> p t i", t=2)),
                     "items")
            dve.wait_ge(it_ready, 1)
            after_read(dve, "items")

            def make_picks(i):
                for t in range(2):
                    col = item_pos[:, t, bass.ds(i, 1)]
                    dve.tensor_scalar(pick[:, t, :], slot_no[:, :, :].rearrange("p a b -> p (a b)"), col, None,
                                      ALU.is_equal).then_inc(pick_ready, 1)
                    dve.tensor_scalar(pick_w[:, t, :], slot_no[:, :, :].rearrange("p a b -> p (a b)"), col,
                                      item_w[:, t, bass.ds(i, 1)], ALU.is_equal, ALU.mult).then_inc(pickw_ready, 1)

            dve.memset(gu_c[:, 0], 0.0)
            dve.memset(slot_w[:, :], 0.0).then_inc(slot_w_ready, 1)
            dve.memset(zeros[:, :], 0.0)
            dve.memset(put[:, :].bitcast(F32), 0.0).then_inc(put_ready, 1)
            make_picks(0)

            def xs_second():
                dve.tensor_tensor(xs[:, :, TOK:2 * TOK], gather_ps[:, :].rearrange("p (k m) -> p k m", k=KC),
                                  xs[:, :, 0:TOK].bitcast(F32), ALU.subtract).then_inc(xs_ready, 1)

            def y_second(h):
                cols = slice(h * NT, (h + 1) * NT)
                dve.scalar_tensor_tensor(out=y_lo[:, cols], in0=mm[h][:, :], scalar=slot_w[:, 0:1],
                                         in1=y_hi[:, cols].bitcast(F32), op0=ALU.mult, op1=ALU.subtract)\
                    .then_inc(ylo_s[h], 1)

            dve.wait_ge(xs_hi_s, 1)
            xs_second()
            ps = await_job(dve, "bias1")
            was_read(dve.tensor_copy(bias_items[:, 8:16, :], ps[:, 0:8 * ICOLS].rearrange("p (f i) -> p f i", f=8)),
                     "bias1")
            dve.wait_ge(tab_ready, 1)
            n_items = dve.value_load(table[0:1, ICOLS:ICOLS + 1], min_val=1, max_val=ITEMS)
            with dve.Fori(0, GROUPS) as g:
                with dve.If(g * GROUP < n_items):
                    with dve.Fori(0, GROUP) as r:
                        i = dve.snap(g * GROUP + r)
                        with dve.If(i < n_items):
                            i4 = dve.snap(i * GU)
                            i12 = dve.snap(i * 2 * SLOTS)
                            def rest(j, pieces=range(2)):
                                for p in pieces:
                                    k = WHOLE + p * PIECE
                                    dve.wait_ge(hi_done, i12 + 2 * j + p + 1)
                                    dve.tensor_tensor(ring_lo[j][:, k:k + PIECE, :], ring[:, j, k:k + PIECE, :],
                                                      w_hi[:, j % HI_BUFS, p].bitcast(F32), ALU.subtract).then_inc(lo_done, 1)

                            def clamp(j):
                                dve.wait_ge(folded, i4 + j + 1)
                                b = gu_b[:, j % 2]
                                dve.tensor_tensor(b, fold_ps[:, (j % 2) * 256:(j % 2) * 256 + 256]
                                                  .rearrange("p (f t) -> p f t", f=4),
                                                  bias_items[:, 4 * j:4 * j + 4, bass.ds(i, 1)].broadcast_to([P, 4, TOK]),
                                                  ALU.add).then_inc(biased, 1)
                                dve.wait_ge(biased, i4 + j + 1)
                                dve.tensor_scalar(gu_c[:, j % 2, 0:2, :], b[:, 0:2, :], LIMIT, None, ALU.min)\
                                    .then_inc(gate_c, 1)
                                dve.tensor_scalar(gu_c[:, j % 2, 2:4, :], b[:, 2:4, :], LIMIT, -LIMIT, ALU.min, ALU.max)\
                                    .then_inc(up_c, 1)

                            def activate(j):
                                dve.wait_ge(sig_done, i4 + j + 1)
                                dve.tensor_tensor(gated[:, j % 2], gu_c[:, j % 2, 0:2, :], sig[:, j % 2], ALU.mult)\
                                    .then_inc(gated_s, 1)
                                dve.wait_ge(gated_s, i4 + j + 1)
                                dve.wait_ge(up_c, i4 + j + 1)
                                dve.scalar_tensor_tensor(out=act_full[:, j % 2], in0=gu_c[:, j % 2, 2:4, :], scalar=1.0,
                                                         in1=gated[:, j % 2], op0=ALU.add, op1=ALU.mult).then_inc(actf, 1)
                                dve.wait_ge(actf, i4 + j + 1)
                                st = act_st[:, 2 * j:2 * j + 2, :]
                                dve.tensor_copy(st[:, :, 0:TOK], act_full[:, j % 2]).then_inc(acth, 1)
                                dve.wait_ge(acth, i4 + j + 1)
                                dve.tensor_tensor(st[:, :, TOK:2 * TOK], act_full[:, j % 2], st[:, :, 0:TOK].bitcast(F32),
                                                  ALU.subtract).then_inc(act_ready, 1)

                            dve.wait_ge(yhi_s[0], i + 1)
                            y_second(0)
                            rest(0)
                            rest(1)
                            dve.wait_ge(yhi_s[1], i + 1)
                            y_second(1)
                            rest(2)
                            rest(3)
                            clamp(0)
                            activate(0)
                            rest(4, (0,))
                            clamp(1)
                            rest(4, (1,))
                            activate(1)
                            clamp(2)
                            activate(2)
                            dve.wait_ge(turned, i + 1)
                            make_picks(i + 1)
                            rest(5, (0,))
                            clamp(3)
                            activate(3)
                            rest(5, (1,))
                            dve.wait_ge(xs_hi_s, i + 2)
                            xs_second()
            dve.wait_ge(yhi_s[0], n_items + 1)
            y_second(0)
            dve.wait_ge(yhi_s[1], n_items + 1)
            y_second(1)
            dve.wait_ge(l_fin, 16)
            for t in range(2):
                dve.wait_ge(scattered, t + 1)
                for h in range(2):
                    cols = slice(h * NT, (h + 1) * NT)
                    dve.tensor_tensor(fin_y[:, t, cols], acc[2 * t + h][:, :], g2_bc[:, cols], ALU.mult)\
                        .then_inc(f_step, 1)
                dve.wait_ge(f_step, 4 * t + 2)
                for h in range(2):
                    cols = slice(h * NT, (h + 1) * NT)
                    dve.tensor_tensor(fin_y[:, t, cols], fin_y[:, t, cols], h1[:, t, cols], ALU.add)\
                        .then_inc(f_step, 1)
            for t in range(2):
                dve.wait_ge(f_root, t + 1)
                dve.reciprocal(rstd_f[:, t:t + 1], rstd_f[:, t:t + 1]).then_inc(f_step, 1)
                dve.wait_ge(f_step, 9 + 2 * t)
                dve.scalar_tensor_tensor(out=fin_y[:, t, :], in0=fin_y[:, t, :], scalar=rstd_f[:, t:t + 1],
                                         in1=fin_n[:, :], op0=ALU.mult, op1=ALU.mult).then_inc(f_step, 1)

        @block.tensor
        def _(pe):
            def tile_landed(t):
                pe.wait_ge(landed[head_slot(t)], 16 * (head_nth(t) + 1))

            def product(ps, lhs, t, cols=slice(0, NT)):
                for k in range(KC):
                    ins = pe.matmul(ps, lhs(k), ring[:, head_slot(t), k, cols], start=(k == 0), stop=(k == KC - 1))
                return ins

            pe.wait_ge(pool_step, at_step["ident"])
            pe.wait_ge(c_silud, 1)
            ps = await_bank(pe, "cT")
            filled(pe.transpose(ps[:, 0:2 * KC], c_rows[:, :], ident[0:2 * KC, 0:2 * KC]), "cT")
            after_read(pe, "cT")
            pe.wait_ge(c_ready, 1)

            def ada(a, lhs):
                t = HEAD_TILES.index(ADA[a])
                tile_landed(t)
                ps = await_bank(pe, f"ada{a}")
                filled(product(ps[:, :], lhs, t), f"ada{a}")

            def ada_sum(a):
                pe.wait_ge(ada_part, KC * (a - 4))
                ps = await_bank(pe, f"ada{a}")
                filled(pe.matmul(ps[:, :], ones[:, :], ring[:, head_slot(HEAD_TILES.index(ADA[a])), 0, :],
                                 start=True, stop=True), f"ada{a}")

            for a in range(4):
                ada(a, lambda k: c_mix[:, k].rearrange("p a b -> p (a b)"))
            ada(4, lambda k: c_all[:, k, :])
            for m in range(4):
                pe.wait_ge(hn_ready, m + 1)
                for half in range(2):
                    ps = await_bank(pe, f"hnT{m}{half}")
                    for k in range(4):
                        ins = pe.transpose(ps[:, k * P:(k + 1) * P], x_mix[:, m, (4 * half + k) * P:(4 * half + k + 1) * P],
                                           ident[:, :])
                    filled(ins, f"hnT{m}{half}")
            after_read(pe, "hnT30")
            after_read(pe, "hnT31")
            pe.wait_ge(l_aa, 16)
            ps = await_bank(pe, "aa")
            for s in range(2):
                for k in range(KC):
                    ins = pe.matmul(ps[0:2 * RANK, s * SEQ:(s + 1) * SEQ], w_aa[:, k, :], hnT[:, s, k, :],
                                    start=(k == 0), stop=(k == KC - 1))
            filled(ins, "aa")
            qk_tile, v_tile, r_tile = (HEAD_TILES.index(("in", col)) for col in (Q0, V0, R0))
            tile_landed(qk_tile)
            for g in range(4):
                ps = await_bank(pe, f"qk{g}")
                if g < 2:
                    filled(product(ps[:, :], tok(g), qk_tile), f"qk{g}")
                else:
                    filled(product(ps[:, 0:QK], tok(g), qk_tile, slice(QK, 2 * QK)), f"qk{g}")
            ada_sum(5)
            ada_sum(6)
            after_read(pe, "aa")
            pe.wait_ge(l_up, 32)
            for g in range(4):
                ps = await_bank(pe, f"z{g}")
                filled(pe.matmul(ps[:, :], aT[:, g * P:(g + 1) * P], up_blk[:, :], start=True, stop=True), f"z{g}")
            tile_landed(v_tile)
            for g in range(4):
                ps = await_bank(pe, f"v{g}")
                filled(product(ps[:, :], tok(g), v_tile), f"v{g}")
            ada_sum(7)
            ada_sum(8)
            pe.wait_ge(pool_step, at_step["scan"])
            for g in range(4):
                pe.wait_ge(la_ready, g + 1)
                ps = await_bank(pe, f"kp{g}")
                for d in range(2):
                    ins = pe.matmul(ps[:, d * QK:(d + 1) * QK], beyond[:, d, :], la[:, g, d * QK:(d + 1) * QK],
                                    start=True, stop=True)
                filled(ins, f"kp{g}")
            ps = await_bank(pe, "dec")
            for g in range(4):
                for dp in range(4):
                    col = 8 * g + 2 * dp
                    ins = pe.matmul(ps[:, col:col + 2], la[:, g, dp * P:(dp + 1) * P], in_chunk[:, :],
                                    start=True, stop=True)
            filled(ins, "dec")
            for t in range(2):
                ps = await_bank(pe, f"bT{t}")
                for dp in range(4):
                    ins = pe.matmul(ps[:, dp * P:(dp + 1) * P], la[:, t, dp * P:(dp + 1) * P], up_to[:, dp // 2, :],
                                    start=True, stop=True)
                filled(ins, f"bT{t}")
            tile_landed(r_tile)
            for t in range(2):
                ps = await_bank(pe, f"r{t}")
                filled(product(ps[:, :], tok(t), r_tile), f"r{t}")
            for t in range(2):
                ps = await_bank(pe, f"qkT{t}")
                for a in range(4):
                    ins = pe.transpose(ps[:, a * P:(a + 1) * P], qk_rows[:, t, a * P:(a + 1) * P], ident[:, :])
                filled(ins, f"qkT{t}")
            def chunk_sums(s):
                for dp in range(4):
                    name = f"kvf{s}" if dp < 2 else f"kvb{s}"
                    ps = await_bank(pe, name) if dp % 2 == 0 else bank[JOBS[name][0]]
                    step = s if s < 4 else s - 4
                    ch = step if dp < 2 else 3 - step
                    g = (2 if s < 4 else 0) + ch // 2
                    rows = slice((ch % 2) * CH, (ch % 2) * CH + CH)
                    for hh in range(2):
                        h = 2 * (dp % 2) + hh
                        ins = pe.matmul(ps[hh * DK:(hh + 1) * DK, dp % 2 * DV:(dp % 2 + 1) * DV],
                                        k_end[rows, g, dp // 2, h * DK:(h + 1) * DK],
                                        v_rows[rows, g, h * DV:(h + 1) * DV], start=True, stop=True,
                                        skip_group_check=True)
                    if dp % 2:
                        filled(ins, name)

            pe.wait_ge(k_ready, 4)
            after_read(pe, "v3")
            after_read(pe, "v2")
            for n, what in enumerate("cxb"):
                t = HEAD_TILES.index(("in", (C0, X0, B0)[n]))
                tile_landed(t)
                for half in range(2):
                    ps = await_bank(pe, f"{what}{half}")
                    for f in range(2):
                        for k in range(KC):
                            ins = pe.matmul(ps[:, f * SEQ:(f + 1) * SEQ],
                                            ring[:, head_slot(t), k, (2 * half + f) * P:(2 * half + f + 1) * P],
                                            hnT[:, 0, k, :], start=(k == 0), stop=(k == KC - 1))
                    filled(ins, f"{what}{half}")
                    chunk_sums(2 * n + half)
                if what == "c":
                    ada_sum(9)
            chunk_sums(6)
            after_read(pe, "qkT1")
            after_read(pe, "qkT0")
            pe.wait_ge(qd_ready, 6)
            for t in range(2):
                for odd, name in enumerate((f"sce{t}", f"sco{t}")):
                    ps = await_bank(pe, name)
                    rows = slice(odd * DK, (odd + 1) * DK)
                    for cc, h, d in [(cc, h, d) for cc in range(2) for h in (odd, odd + 2) for d in range(2)]:
                            toks = slice(t * P + cc * CH, t * P + cc * CH + CH)
                            col = (2 * (h // 2) + d) * CH
                            ins = pe.matmul(ps[cc * CH:(cc + 1) * CH, col:col + CH],
                                            k_inv[rows, 2 * d + h // 2, toks], q_dec[rows, 2 * d + h // 2, toks],
                                            start=True, stop=True, skip_group_check=True)
                    filled(ins, name)
            after_read(pe, "kvf6")
            after_read(pe, "kvb6")
            for t in range(2):
                after_read(pe, f"sce{t}")
                after_read(pe, f"sco{t}")
                within = await_bank(pe, f"oi{t}")
                for cc in range(2):
                    rows = slice(cc * CH, (cc + 1) * CH)
                    for h in range(HEADS):
                        for d in range(2):
                            ins = pe.matmul(within[rows, h * DV:(h + 1) * DV], scores[rows, t, h, d, :],
                                            v_rows[rows, t, h * DV:(h + 1) * DV], start=(d == 0), stop=(d == 1),
                                            skip_group_check=True)
                filled(ins, f"oi{t}")
                for odd, name in enumerate((f"oe{t}", f"oo{t}")):
                    before = await_bank(pe, name)
                    rows = slice(odd * DK, (odd + 1) * DK)
                    for cc in range(2):
                        toks = slice(t * P + cc * CH, t * P + cc * CH + CH)
                        for hp in range(2):
                            for d in range(2):
                                ins = pe.matmul(before[cc * CH:(cc + 1) * CH, hp * DV:(hp + 1) * DV],
                                                q_dec[rows, 2 * d + hp, toks], states[rows, 2 * d + hp, 2 * t + cc, :],
                                                start=(d == 0), stop=(d == 1), skip_group_check=True)
                    filled(ins, name)
            ada(10, lambda k: c_all[:, k, :])
            for t in range(2):
                pe.wait_ge(y_ready, t + 1)
                ps = await_bank(pe, f"yT{t}")
                for f in range(4):
                    ins = pe.transpose(ps[:, f * P:(f + 1) * P], o_rows[:, t, f * P:(f + 1) * P], ident[:, :])
                filled(ins, f"yT{t}")
            after_read(pe, "yT0")
            after_read(pe, "yT1")
            pe.wait_ge(yconv, 2)
            for half in range(2):
                t_out = HEAD_TILES.index(("out", NT * half))
                tile_landed(t_out)
                for t in range(2):
                    ps = await_bank(pe, f"wo{half}{t}")
                    filled(product(ps[:, :], lambda k: yT[:, k, t * P:(t + 1) * P], t_out), f"wo{half}{t}")
            ada(11, lambda k: c_all[:, k, :])
            for t in range(2):
                pe.wait_ge(hn2_ready, t + 1)
                for half in range(2):
                    ps = await_bank(pe, f"h2T{t}{half}")
                    for k in range(4):
                        ins = pe.transpose(ps[:, k * P:(k + 1) * P], hn2[:, t, (4 * half + k) * P:(4 * half + k + 1) * P],
                                           ident[:, :])
                    filled(ins, f"h2T{t}{half}")
            for t in range(2):
                for half in range(2):
                    after_read(pe, f"h2T{t}{half}")
            pe.wait_ge(l_router, 32)
            ps = await_bank(pe, "logits")
            for t in range(2):
                for k in range(KC):
                    ins = pe.matmul(ps[:, t * E:(t + 1) * E], h2T[:, k, t * P:(t + 1) * P], r_w[:, k, :],
                                    start=(k == 0), stop=(k == KC - 1))
            filled(ins, "logits")
            pe.wait_ge(rt_sel, 1)
            pe.wait_ge(pool_step, at_step["tables"])
            ps = await_bank(pe, "rank")
            pe.matmul(ps[:, 0:E], tri[:, :], sel[:, 0, :], start=True, stop=True)
            pe.matmul(ps[:, E:2 * E], tri[:, :], sel[:, 1, :], start=True, stop=False)
            pe.matmul(ps[:, E:2 * E], ones[:, :], sel[:, 0, :], start=False, stop=True)
            for t in range(2):
                ins = pe.matmul(ps[0:E, 64:65], sel[:, t, :], ones[:, 0:1], start=(t == 0), stop=(t == 1))
            filled(ins, "rank")
            pe.wait_ge(rt_pos, 2)
            ps = await_bank(pe, "turn")
            for n, src in enumerate((pos, w_full)):
                for t in range(2):
                    ins = pe.transpose(ps[0:E, (2 * n + t) * P:(2 * n + t + 1) * P], src[:, t, :], ident[:, :])
            filled(ins, "turn")
            after_read(pe, "rank")
            ps = await_bank(pe, "start")
            pe.matmul(ps[0:E, 0:1], below[:, :], tiles_e[:, :], start=True, stop=True)
            filled(pe.matmul(ps[0:1, 1:2], tiles_e[:, :], ones[0:E, 0:1], start=True, stop=True), "start")
            pe.wait_ge(rt_own, 6)
            pe.wait_ge(rt_T, 1)
            after_read(pe, "turn")
            ps = await_bank(pe, "items")
            for n in range(2):
                for t in range(2):
                    col = (2 * n + t) * ICOLS
                    pe.matmul(ps[:, col:col + ICOLS], routeT[:, n, t * P:(t + 1) * P], own[:, :], start=True, stop=True)
            filled(pe.matmul(ps[0:1, 4 * ICOLS:5 * ICOLS], e_col[:, :], own[:, :], start=True, stop=True), "items")
            def gather():
                for k in range(KC):
                    for t in range(2):
                        for part in range(3):
                            ins = pe.matmul(gather_ps[:, k * TOK:(k + 1) * TOK], hn2_parts[:, t, part, k * P:(k + 1) * P],
                                            pick[:, t, 0:TOK], start=(t == 0 and part == 0),
                                            stop=(t == 1 and part == 2))
                ins.then_inc(gathered, 1)

            def scatter(last):
                for t in range(2):
                    for h in range(2):
                        for n, src in enumerate((y_hi, y_lo)):
                            ins = pe.matmul(acc[2 * t + h][:, :], put[:, t * P:(t + 1) * P],
                                            src[:, h * NT:(h + 1) * NT], start=False, stop=(last and n == 1),
                                            skip_group_check=True)
                    if last:
                        ins.then_inc(scattered, 1)

            def biases(half):
                ps = await_bank(pe, f"bias{half}")
                for n in range(8):
                    j, part = (8 * half + n) // 4, (8 * half + n) % 4
                    first = 2 * P * (2 * j + part % 2) + part // 2
                    ins = pe.matmul(ps[:, n * ICOLS:(n + 1) * ICOLS], bgu_rows[:, first:first + 2 * P - 1:2], own[:, :],
                                    start=True, stop=True)
                filled(ins, f"bias{half}")

            for j in range(SLOTS):
                pe.nop().then_inc(used[j], 1)
            pe.wait_ge(l_bgu, 16)
            biases(0)
            pe.wait_ge(pick_ready, 2)
            pe.wait_ge(part_c, 2)
            pe.wait_ge(part_r, 3)
            gather()
            biases(1)
            pe.wait_ge(put_ready, 1)
            for name in ("rank", "turn", "items", "bias0", "ada10", "ada11"):
                after_read(pe, name)
            for b in range(4):
                for n in range(0, NT, P):
                    pe.matmul(acc[b][:, n:n + P], zeros[:, :], ident_bf[:, :], start=True, stop=False,
                              skip_group_check=True)
            pe.wait_ge(tab_ready, 1)
            after_read(pe, "bias1")
            n_items = pe.value_load(table[0:1, ICOLS:ICOLS + 1], min_val=1, max_val=ITEMS)
            with pe.Fori(0, GROUPS) as g:
                with pe.If(g * GROUP < n_items):
                    with pe.Fori(0, GROUP) as r:
                        i = pe.snap(g * GROUP + r)
                        with pe.If(i < n_items):
                            i4 = pe.snap(i * GU)
                            i12 = pe.snap(i * 2 * SLOTS)
                            def whole(j, lhs, chunks):
                                for k in chunks:
                                    pe.matmul(mm[j % 2][:, :], lhs[:, k, :].bitcast(F32), ring[:, j, k, :],
                                              start=(k == 0), stop=False)

                            def split(j, lhs):
                                for p in range(2):
                                    pe.wait_ge(lo_done, i12 + 2 * j + p + 1)
                                    if j == 4:
                                        pe.wait_ge(act_ready, i4 + 3 + p)
                                    for s in range(PIECE):
                                        k = WHOLE + p * PIECE + s
                                        for n, half in enumerate((w_hi[:, j % HI_BUFS, p, s, :], ring_lo[j][:, k, :])):
                                            ins = pe.matmul(mm[j % 2][:, :], lhs[:, k, :], half,
                                                            start=False, stop=(k == KC - 1 and n == 1))
                                ins.then_inc(used[j], 1)

                            def gate_up(j):
                                pe.wait_ge(landed[j], 16 * (i + HEAD_USES[j] + 1))
                                if j < 2:
                                    pe.wait_ge(ylo_s[j], i + 1)
                                else:
                                    pe.wait_ge(rows_out, i4 + j - 1)
                                whole(j, xs, range(WHOLE))
                                split(j, xs)

                            def fold_rows(j):
                                pe.wait_ge(rows_out, i4 + j + 1)
                                if j:
                                    pe.wait_ge(biased, i4 + j)
                                for part in range(4):
                                    first = 2 * P * (2 * j + part % 2) + part // 2
                                    col = (j % 2) * 256 + part * TOK
                                    ins = pe.matmul(fold_ps[:, col:col + TOK], gu_rows[:, first:first + 2 * P - 1:2],
                                                    fold[:, :], start=True, stop=True)
                                ins.then_inc(folded, 1)

                            pe.wait_ge(xs_ready, i + 1)
                            gate_up(0)
                            gate_up(1)
                            fold_rows(0)
                            gate_up(2)
                            fold_rows(1)
                            pe.wait_ge(put_ready, i + 1)
                            pe.wait_ge(ylo_s[0], i + 1)
                            pe.wait_ge(ylo_s[1], i + 1)
                            scatter(False)
                            pe.wait_ge(pick_ready, 2 * i + 2)
                            pe.wait_ge(pickw_ready, 2 * i + 2)
                            for t in range(2):
                                pe.matmul(gather_ps[:, t * P:(t + 1) * P], pick[:, t, :], ident_bf[:, :],
                                          start=True, stop=True)
                            for t in range(2):
                                ins = pe.matmul(gather_ps[:, SEQ:SEQ + 1], pick_w[:, t, :], ones[:, 0:1],
                                                start=(t == 0), stop=(t == 1))
                            ins.then_inc(turned, 1)
                            fold_rows(2)
                            gate_up(3)
                            pe.wait_ge(landed[4], 16 * (i + HEAD_USES[4] + 1))
                            pe.wait_ge(act_ready, i4 + 1)
                            whole(4, act_st, (0,))
                            fold_rows(3)
                            whole(4, act_st, range(1, WHOLE))
                            pe.wait_ge(pick_ready, 2 * i + 4)
                            pe.wait_ge(put_ready, i + 2)
                            pe.wait_ge(slot_w_ready, i + 2)
                            gather()
                            split(4, act_st)
                            pe.wait_ge(landed[5], 16 * (i + HEAD_USES[5] + 1))
                            whole(5, act_st, range(WHOLE))
                            split(5, act_st)
            pe.wait_ge(l_bdn, 16)
            for t in range(2):
                for h in range(2):
                    pe.matmul(acc[2 * t + h][:, :], routeT[:, 1, t * P:(t + 1) * P], bdn_rows[:, h * NT:(h + 1) * NT],
                              start=False, stop=False, skip_group_check=True)
            pe.wait_ge(put_ready, n_items + 1)
            pe.wait_ge(ylo_s[0], n_items + 1)
            pe.wait_ge(ylo_s[1], n_items + 1)
            scatter(True)


_INS = ['x', 'c', 'ctx', 'c_ctx', 'w_ada', 'b_ada', 'norm1_w', 'w_in', 'a_up_f', 'a_bias_f', 'a_up_b', 'a_bias_b',
        'gla_norm_w', 'conv_w', 'w_out', 'norm2_w', 'router_w', 'router_b', 'w_gu', 'b_gu', 'w_dn', 'b_dn',
        'final_norm_w']
_OUTS = [((1, 256, 1024), 'float32')]


def kernel(**inputs):
    import numpy as _np
    import concourse.bacc as _bacc
    from concourse import mybir as _mybir
    from concourse.bass_utils import run_bass_kernel_spmd as _run

    nc = _bacc.Bacc("TRN2", target_bir_lowering=False, num_devices=1)
    arrays, args = {}, []
    for name in _INS:
        a = _np.ascontiguousarray(inputs[name])
        arrays[f"in_{name}_dram"] = a
        args.append(nc.dram_tensor(f"in_{name}_dram", a.shape, _mybir.dt.from_np(a.dtype), kind="ExternalInput").ap())
    for i, (shape, dtype) in enumerate(_OUTS):
        dt = _mybir.dt.from_np(_np.dtype(dtype))
        args.append(nc.dram_tensor(f"out_{i}_dram", shape, dt, kind="ExternalOutput").ap())
    hybrid_layer(nc, *args)
    r = _run(nc, [arrays], core_ids=[0])
    got = tuple(r.results[0][f"out_{i}_dram"] for i in range(len(_OUTS)))
    return got[0]
```
